# Optimizing a Trainium2 kernel written in Bass

```python
import jax, jax.numpy as jnp
from jax import lax
import numpy as np

D_MODEL = 1024
BATCH = 1
SEQ = 256
DEPTH = 2

HEAD_DIM = 64
RW_HEADS = 8
RW_WIDTH = RW_HEADS * HEAD_DIM
RW_DECAY_LORA = 64
RW_A_LORA = 64
RW_V_LORA = 32
RW_G_LORA = 128
RW_GN_EPS = 64e-5
FOX_HEADS = 8
FOX_WIDTH = FOX_HEADS * HEAD_DIM
MLA_HEADS = 8
MLA_NOPE = 64
MLA_ROPE = 32
MLA_V = 64
MLA_Q_LORA = 256
MLA_KV_LORA = 256
ROPE_BASE = 10000.0
N_BRANCH = 3
BRANCH_WIDTH = 512
D_FF = 2816
CONV_WIDTH = 3
Q_BLOCK = 128
NORM_EPS = 1e-6

RW_SIZES = (RW_WIDTH, RW_DECAY_LORA, RW_WIDTH, RW_WIDTH, RW_A_LORA, RW_G_LORA)
RW_COLS = 3 * RW_WIDTH + RW_DECAY_LORA + RW_A_LORA + RW_G_LORA
REST_SIZES = (FOX_WIDTH, FOX_WIDTH, FOX_WIDTH, FOX_HEADS,
              MLA_Q_LORA, MLA_KV_LORA, MLA_ROPE, N_BRANCH * D_MODEL)
N_IN_COLS = RW_COLS + 3 * FOX_WIDTH + FOX_HEADS + MLA_Q_LORA + MLA_KV_LORA + MLA_ROPE + N_BRANCH * D_MODEL

kernel_name = 'hybrid_rwkv7_fox_mla_convffn_adaln'

def rms_norm(x, g, eps=NORM_EPS):
    xf = x.astype(jnp.float32)
    y = xf * lax.rsqrt(jnp.mean(xf * xf, axis=-1, keepdims=True) + eps)
    return (y * g.astype(jnp.float32)).astype(x.dtype)

def split_cols(p, sizes):
    idx, acc = [], 0
    for s in sizes[:-1]:
        acc += s
        idx.append(acc)
    return jnp.split(p, idx, axis=-1)

def token_shift_mix(p, mu):
    prev = jnp.pad(p, ((0, 0), (1, 0), (0, 0)))[:, :-1]
    return p + (prev - p) * mu

def apply_rope(t, positions):
    half = t.shape[-1] // 2
    inv_freq = jnp.power(ROPE_BASE, -jnp.arange(half, dtype=jnp.float32) / half)
    ang = positions.astype(jnp.float32)[:, :, None, None] * inv_freq
    cos, sin = jnp.cos(ang), jnp.sin(ang)
    tf = t.astype(jnp.float32)
    t1, t2 = tf[..., :half], tf[..., half:]
    return jnp.concatenate([t1 * cos - t2 * sin, t1 * sin + t2 * cos], axis=-1).astype(t.dtype)

def causal_block_attention(q, k, v, scale, log_f_cum=None):
    T = q.shape[2]
    outs = []
    for blk in range(T // Q_BLOCK):
        q0 = blk * Q_BLOCK
        L = q0 + Q_BLOCK
        s = jnp.einsum('bhqd,bhkd->bhqk', q[:, :, q0:L], k[:, :, :L]).astype(jnp.float32) * scale
        if log_f_cum is not None:
            s = s + log_f_cum[:, :, q0:L, None] - log_f_cum[:, :, None, :L]
        causal = (q0 + jnp.arange(Q_BLOCK))[:, None] >= jnp.arange(L)[None, :]
        s = jnp.where(causal, s, -jnp.inf)
        p = jax.nn.softmax(s, axis=-1).astype(v.dtype)
        outs.append(jnp.einsum('bhqk,bhkd->bhqd', p, v[:, :, :L]))
    return jnp.concatenate(outs, axis=2)

def rwkv7_time_mix(r, wl, k, v, al, gl, w_up, w0, a_up, a0, g_up, k_k, k_a, r_k, gn_w, gn_b,
                   v_first, vres):
    B, T, _ = r.shape
    H, N = RW_HEADS, HEAD_DIM
    f32 = jnp.float32
    w = -jax.nn.softplus(-(w0 + jnp.tanh(wl) @ w_up).astype(f32)) - 0.5
    decay = jnp.exp(-jnp.exp(w))
    a = jax.nn.sigmoid(a0 + al @ a_up)
    g = jax.nn.sigmoid(gl) @ g_up
    if vres is not None:
        lv, v_up, v0 = vres
        v = v + (v_first - v) * jax.nn.sigmoid(v0 + lv @ v_up)
    kk = (k * k_k).reshape(B, T, H, N).astype(f32)
    kk = kk * lax.rsqrt(jnp.maximum(jnp.sum(kk * kk, axis=-1, keepdims=True), 1e-24))
    k = k * (1 + (a - 1) * k_a)

    def heads_tm(t):
        return jnp.moveaxis(t.reshape(B, T, H, N).astype(f32), 1, 0)

    xs = (heads_tm(r), heads_tm(decay), heads_tm(k), heads_tm(v), jnp.moveaxis(kk, 1, 0), heads_tm(a))

    def step(S, inp):
        r_t, d_t, k_t, v_t, kk_t, a_t = inp
        s_kk = jnp.einsum('bhvk,bhk->bhv', S, kk_t)
        S = (S * d_t[:, :, None, :]
             - s_kk[..., None] * (kk_t * a_t)[:, :, None, :]
             + v_t[..., None] * k_t[:, :, None, :])
        return S, jnp.einsum('bhvk,bhk->bhv', S, r_t)

    _, y = lax.scan(step, jnp.zeros((B, H, N, N), f32), xs)
    y = jnp.moveaxis(y, 0, 1)
    mu = jnp.mean(y, axis=-1, keepdims=True)
    var = jnp.mean(jnp.square(y - mu), axis=-1, keepdims=True)
    y = (y - mu) * lax.rsqrt(var + RW_GN_EPS)
    y = y * gn_w.reshape(H, N).astype(f32) + gn_b.reshape(H, N).astype(f32)
    bonus = jnp.sum((r * k * r_k).reshape(B, T, H, N).astype(f32), axis=-1, keepdims=True)
    y = y + bonus * v.reshape(B, T, H, N).astype(f32)
    return y.reshape(B, T, H * N).astype(r.dtype) * g, v

def fox_attention(q, k, v, f_logit, b_f):
    B, T, _ = q.shape

    def heads(t):
        return t.reshape(B, T, FOX_HEADS, HEAD_DIM).transpose(0, 2, 1, 3)

    log_f = jax.nn.log_sigmoid((f_logit + b_f).astype(jnp.float32))
    cum = jnp.cumsum(log_f, axis=1).transpose(0, 2, 1)
    o = causal_block_attention(heads(q), heads(k), heads(v), HEAD_DIM ** -0.5, cum)
    return o.transpose(0, 2, 1, 3).reshape(B, T, FOX_WIDTH)

def mla_attention(q_lat, kv_lat, k_rope, positions, q_norm_g, w_q_up, kv_norm_g, w_kv_up):
    B, T, _ = q_lat.shape
    H = MLA_HEADS
    q = (rms_norm(q_lat, q_norm_g) @ w_q_up).reshape(B, T, H, MLA_NOPE + MLA_ROPE)
    kv = (rms_norm(kv_lat, kv_norm_g) @ w_kv_up).reshape(B, T, H, MLA_NOPE + MLA_V)
    q_nope, q_pe = q[..., :MLA_NOPE], apply_rope(q[..., MLA_NOPE:], positions)
    k_nope, v = kv[..., :MLA_NOPE], kv[..., MLA_NOPE:]
    k_pe = jnp.broadcast_to(apply_rope(k_rope[:, :, None, :], positions), (B, T, H, MLA_ROPE))
    q = jnp.concatenate([q_nope, q_pe], axis=-1).transpose(0, 2, 1, 3)
    k = jnp.concatenate([k_nope, k_pe], axis=-1).transpose(0, 2, 1, 3)
    o = causal_block_attention(q, k, v.transpose(0, 2, 1, 3), (MLA_NOPE + MLA_ROPE) ** -0.5)
    return o.transpose(0, 2, 1, 3).reshape(B, T, H * MLA_V)

def conv_ffn(h, w_up, conv_w, conv_b, w_down):
    u = h @ w_up
    C = u.shape[-1]
    u = lax.conv_general_dilated(u, conv_w[:, None, :], window_strides=(1,),
                                 padding=((CONV_WIDTH - 1, 0),),
                                 dimension_numbers=('NWC', 'WIO', 'NWC'),
                                 feature_group_count=C) + conv_b
    ug, uv = jnp.split(u, 2, axis=-1)
    return (jax.nn.silu(ug) * uv) @ w_down

def setup_inputs(seed: int = 0) -> dict:
    key = jax.random.key(seed)
    ks = iter(jax.random.split(key, 48))
    L, D = DEPTH, D_MODEL

    def nrm(shape, scale):
        return jax.random.normal(next(ks), shape, jnp.float32) * scale

    def unif(shape, lo, hi):
        return jax.random.uniform(next(ks), shape, jnp.float32, lo, hi)

    x = nrm((BATCH, SEQ, D), 1.0)
    c = nrm((BATCH, D), 1.0)
    offset = jax.random.randint(next(ks), (BATCH, 1), 0, 2048, jnp.int32)
    positions = offset + jnp.arange(SEQ, dtype=jnp.int32)[None, :]
    return {
        'x': x, 'c': c, 'positions': positions,
        'norm1_g': 1.0 + nrm((L, D), 0.02),
        'norm2_g': 1.0 + nrm((L, D), 0.02),
        'w_ada': nrm((L, D, 6 * D), 0.5 * D ** -0.5),
        'b_ada': nrm((L, 6 * D), 0.02),
        'w_in': nrm((L, D, N_IN_COLS), D ** -0.5),
        'mu_shift': unif((L, RW_COLS), 0.0, 1.0),
        'rw_w_up': nrm((L, RW_DECAY_LORA, RW_WIDTH), 0.1 * RW_DECAY_LORA ** -0.5),
        'rw_w0': unif((L, RW_WIDTH), -6.0, -1.0),
        'rw_a_up': nrm((L, RW_A_LORA, RW_WIDTH), RW_A_LORA ** -0.5),
        'rw_a0': nrm((L, RW_WIDTH), 0.1),
        'rw_g_up': nrm((L, RW_G_LORA, RW_WIDTH), RW_G_LORA ** -0.5),
        'rw_k_k': 0.85 + nrm((L, RW_WIDTH), 0.05),
        'rw_k_a': 1.0 + nrm((L, RW_WIDTH), 0.05),
        'rw_r_k': nrm((L, RW_WIDTH), 0.1),
        'rw_gn_w': 1.0 + nrm((L, RW_WIDTH), 0.02),
        'rw_gn_b': nrm((L, RW_WIDTH), 0.02),
        'rw_vres_down': nrm((L - 1, D, RW_V_LORA), D ** -0.5),
        'rw_vres_mu': unif((L - 1, RW_V_LORA), 0.0, 1.0),
        'rw_vres_up': nrm((L - 1, RW_V_LORA, RW_WIDTH), RW_V_LORA ** -0.5),
        'rw_v0': nrm((L - 1, RW_WIDTH), 0.1),
        'fox_b_f': unif((L, FOX_HEADS), 1.0, 4.0),
        'mla_q_norm_g': 1.0 + nrm((L, MLA_Q_LORA), 0.02),
        'mla_w_q_up': nrm((L, MLA_Q_LORA, MLA_HEADS * (MLA_NOPE + MLA_ROPE)), MLA_Q_LORA ** -0.5),
        'mla_kv_norm_g': 1.0 + nrm((L, MLA_KV_LORA), 0.02),
        'mla_w_kv_up': nrm((L, MLA_KV_LORA, MLA_HEADS * (MLA_NOPE + MLA_V)), MLA_KV_LORA ** -0.5),
        'w_branch': nrm((L, N_BRANCH, BRANCH_WIDTH, D), BRANCH_WIDTH ** -0.5),
        'w_o': nrm((L, D, D), D ** -0.5),
        'ffn_w_up': nrm((L, D, 2 * D_FF), D ** -0.5),
        'ffn_conv_w': nrm((L, CONV_WIDTH, 2 * D_FF), CONV_WIDTH ** -0.5),
        'ffn_conv_b': nrm((L, 2 * D_FF), 0.02),
        'ffn_w_down': nrm((L, D_FF, D), D_FF ** -0.5),
        'final_g': 1.0 + nrm((D,), 0.02),
    }

def reference(x, c, positions, norm1_g, norm2_g, w_ada, b_ada, w_in, mu_shift,
              rw_w_up, rw_w0, rw_a_up, rw_a0, rw_g_up, rw_k_k, rw_k_a, rw_r_k, rw_gn_w, rw_gn_b,
              rw_vres_down, rw_vres_mu, rw_vres_up, rw_v0, fox_b_f,
              mla_q_norm_g, mla_w_q_up, mla_kv_norm_g, mla_w_kv_up,
              w_branch, w_o, ffn_w_up, ffn_conv_w, ffn_conv_b, ffn_w_down, final_g):
    B, T, D = x.shape
    c_act = jax.nn.silu(c)
    v_first = None
    for i in range(DEPTH):
        mod = (c_act @ w_ada[i] + b_ada[i])[:, None, :]
        sh1, sc1, g1, sh2, sc2, g2 = jnp.split(mod, 6, axis=-1)

        h = rms_norm(x, norm1_g[i]) * (1 + sc1) + sh1
        w_cat = w_in[i] if i == 0 else jnp.concatenate([w_in[i], rw_vres_down[i - 1]], axis=1)
        proj = h @ w_cat
        rw_part = token_shift_mix(proj[..., :RW_COLS], mu_shift[i])
        r, wl, k, v, al, gl = split_cols(rw_part, RW_SIZES)
        fq, fk, fv, ff, mq, mkv, mkr, gate_logits = split_cols(proj[..., RW_COLS:N_IN_COLS], REST_SIZES)
        if i == 0:
            vres = None
        else:
            vres = (token_shift_mix(proj[..., N_IN_COLS:], rw_vres_mu[i - 1]), rw_vres_up[i - 1], rw_v0[i - 1])

        y_rw, v_rw = rwkv7_time_mix(r, wl, k, v, al, gl, rw_w_up[i], rw_w0[i], rw_a_up[i], rw_a0[i],
                                    rw_g_up[i], rw_k_k[i], rw_k_a[i], rw_r_k[i], rw_gn_w[i], rw_gn_b[i],
                                    v_first, vres)
        if i == 0:
            v_first = v_rw
        y_fox = fox_attention(fq, fk, fv, ff, fox_b_f[i])
        y_mla = mla_attention(mq, mkv, mkr, positions, mla_q_norm_g[i], mla_w_q_up[i],
                              mla_kv_norm_g[i], mla_w_kv_up[i])

        branches = jnp.stack([y_rw, y_fox, y_mla], axis=2)
        branch_d = jnp.einsum('btgc,gcd->btgd', branches, w_branch[i])
        gates = jax.nn.sigmoid(gate_logits).reshape(B, T, N_BRANCH, D)
        mixed = jnp.sum(gates * branch_d, axis=2) @ w_o[i]
        x = x + g1 * mixed

        h = rms_norm(x, norm2_g[i]) * (1 + sc2) + sh2
        x = x + g2 * conv_ffn(h, ffn_w_up[i], ffn_conv_w[i], ffn_conv_b[i], ffn_w_down[i])
    return rms_norm(x, final_g)


_drawn_inputs = setup_inputs


def setup_inputs(seed=0):
    import zlib

    import numpy as np

    out = dict(_drawn_inputs(seed))
    spreads = {}
    factors = {'norm1_g': 8.0,
     'norm2_g': 47.385,
     'rw_w_up': 64.0,
     'rw_a0': 8.0,
     'rw_k_k': 200.0,
     'rw_k_a': 5.805,
     'rw_gn_w': 200.0,
     'rw_gn_b': 200.0,
     'rw_vres_mu': 3.853,
     'rw_v0': 28.959,
     'fox_b_f': 106.472,
     'mla_q_norm_g': 64.0,
     'mla_kv_norm_g': 64.0,
     'ffn_conv_b': 49.805,
     'final_g': 23.024,
     'rw_w0': 4.03}
    for name, (base, spread) in spreads.items():
        noise = np.random.default_rng([zlib.crc32(name.encode()), seed]).standard_normal(out[name].shape)
        drawn = base * np.exp(spread * noise) if base else spread * noise
        out[name] = __import__('jax').numpy.asarray(drawn.astype(out[name].dtype))
    for name, factor in factors.items():
        out[name] = (out[name] * factor).astype(out[name].dtype)
    return out
```

```python
from contextlib import ExitStack

import numpy as np

import concourse.bass as bass
from concourse import mybir

F32 = mybir.dt.float32
I32 = mybir.dt.int32
ALU = mybir.AluOpType
ACT = mybir.ActivationFunctionType

P = 128
D_MODEL, SEQ, DEPTH = 1024, 256, 2
KT = D_MODEL // P
TB = SEQ // P
H, HD = 8, 64
NOPE, ROPE = 64, 32
D_FF = 2816
FT = D_FF // P
CHUNK = 64
NCH = SEQ // CHUNK
UNIT = 1024
RING = 3
AHEAD = 2

T_MIX, T_WA, T_GL, T_R, T_K, T_V, T_MQ, T_MKV, T_FQ, T_FK = 0, 1, 2, 3, 7, 11, 15, 17, 19, 23
N_FEAT = 27

U_LORA, U_FV, U_QUP, U_KUP, U_VUP = 19, 29, 33, 35, 36
U_GB = 37
U_GR, U_BR, U_WO, U_FF = 61, 69, 73, 81
N_UNITS = U_FF + 3 * FT
assert N_UNITS % RING == 0

C_N1, C_N2, C_BADA, C_MU, C_W0, C_A0, C_V0 = 0, 8, 16, 64, 79, 83, 87
C_KK, C_KA, C_RK, C_GW, C_GB, C_MIX, C_MQ, C_MKV, C_FLAG = 91, 95, 99, 103, 107, 111, 112, 114, 116
C_CW, C_CB = 120, 252
N_PAR = 296

LEVELS = [2, 4, 8, 16, 32]
K_ID, K_ONES, K_BLK = 0, 128, 384
K_MS, K_MI, K_N2T, K_N2, K_OFF = 512, 640, 768, 896, 1024
K_CAUS, K_RST, K_TRIG, K_FG = 1664, 1920, 2176, 2180
N_CON = 2188

NEG = -1e30
RSQ_E = 0.6065306597126334
TWO_PI = 6.283185307179586
PI2_A, PI2_B = 6.28125, 0.0019350051879882812
PI2_C = TWO_PI - PI2_A - PI2_B
MAGIC = 12582912.0

ADA_UNITS = 16

def rk_order():
    mm, ev = ["ksq", "bonus"], ["ready", "bon", "rho"]
    for b in range(TB):
        mm.append(f"tr{b}")
        ev.append(f"tr{b}")
        for par in range(2):
            g = f"{b}{par}"
            mm += [f"S{g}", f"LV{g}"]
            ev.append(f"S{g}")
            for i in range(len(LEVELS)):
                mm += [f"X{g}{i}"] + [f"T{g}{i}"] * (i < len(LEVELS) - 1) + [f"TT{g}{i}"]
                ev += [f"X{g}{i}", f"TT{g}{i}"]
            mm += [f"WU{g}", f"ZG{g}"]
            ev += [f"WU{g}", f"ZG{g}"]
    mm += [f"st{q}" for q in range(1, NCH - 1)] + ["y", "mean", "var"]
    ev += [f"st{q}" for q in range(NCH - 1)] + ["y", "mean", "var"]
    return [{n: i + 1 for i, n in enumerate(names)} for names in (mm, ev)]


RK_MM, RK_EV = rk_order()
N_MM, N_EV = len(RK_MM), len(RK_EV)


def up_unit(j):
    return U_FF + 2 * j if j < 2 else U_FF + 4 + 3 * (j - 2)


def down_unit(j):
    return U_FF + 6 + 3 * j if j < FT - 2 else N_UNITS - FT + j


A_UNITS = (list(range(U_FV)) + [U_FV + 1, U_FV + 3] + [u for u in range(U_GB, U_GR) if (u - U_GB) % 3 < 2]
           + list(range(U_GR, U_BR)))
V_UNITS = list(range(U_GB + 2, U_GR, 3)) + list(range(U_BR, U_FF))
A_PLACE = {u: i + 1 for i, u in enumerate(A_UNITS)}
V_PLACE = {u: i + 1 for i, u in enumerate(V_UNITS)}
N_A, N_V = len(A_UNITS), len(V_UNITS)

N_SPLIT = 5
S_LORA, S_LAT, S_FOX, S_MLA, S_RW = 1, 2, 3, 4, 5
N_H = 20
H_N1, H_MG, H_N2 = 0, 8, 12
N_NORM = 3
N_T = 5 * 2 * TB
F32R = mybir.dt.float32r


def bass_trunk(nc, xT, cT, pos, par, con, wada, ws, out):
    ctx = ExitStack()
    with ctx:
        def sb(name, shape, dt=F32):
            return ctx.enter_context(nc.sbuf_tensor(name, shape, dt))

        def sem(name):
            return ctx.enter_context(nc.semaphore(name))

        raw = sb("raw", [P, RING, UNIT])
        wh = sb("wh", [P, RING, UNIT], F32R)
        wl = sb("wl", [P, RING, UNIT], F32R)
        x = sb("x", [P, KT, SEQ])
        hh = sb("hh", [P, KT, SEQ], F32R)
        hl = sb("hl", [P, KT, SEQ], F32R)
        sh = sb("sh", [P, 4, SEQ], F32R)
        sl = sb("sl", [P, 4, SEQ], F32R)
        proj = sb("proj", [P, N_FEAT, SEQ + 1])
        vf = sb("vf", [P, TB, 512])
        y = sb("y", [P, 12, SEQ])
        v1st = sb("v1st", [P, 4, SEQ])
        parall = sb("parall", [P, DEPTH, N_PAR])
        pr = sb("pr", [P, N_PAR])
        cn = sb("cn", [P, N_CON])
        mod = sb("mod", [P, 48])
        gain = sb("gain", [P, KT])
        ka1 = sb("ka1", [P, 4])
        cc = sb("cc", [P, KT])
        csig = sb("csig", [P, KT])
        rs = sb("rs", [P, 2, SEQ])
        posi = sb("posi", [P, SEQ], I32)
        trig = sb("trig", [P, SEQ])
        pc = sb("pc", [P, 4, NCH])
        mx, nb, den, rd = (sb(n, [P, 2, 2]) for n in ("mx", "nb", "den", "rd"))
        un = sb("un", [P, 9216])
        prep = sb("prep", [P, 9984])

        def view(t, at, *shape):
            n = int(np.prod(shape))
            v = t[:, at:at + n]
            if len(shape) == 1:
                return v
            if len(shape) == 2:
                return v.rearrange("p (a b) -> p a b", a=shape[0])
            return v.rearrange("p (a b c) -> p a b c", a=shape[0], b=shape[1])

        sq = view(un, 0, KT, SEQ)
        ada = (view(un, 2048, 2048), view(un, 6144, 2048))
        acc = view(un, 4096, 2048)
        shd = view(un, 6144, 3, SEQ)
        fac, sqk = view(un, 6144, 4, SEQ), view(un, 7168, 4, SEQ)
        vt = view(un, 8192, 4, SEQ)
        cum, tmp, kkn = (view(prep, i * 1024, 4, SEQ) for i in range(3))
        lgd, aa, kap, gg = (view(prep, 3072 + i * 1024, 4, SEQ) for i in range(4))
        tw = view(prep, 3072, 2, SEQ)
        bon, bet = lgd, aa
        ar = prep[:, 7168:9216].rearrange("p (m b e t) -> p m b e t", m=4, b=TB, e=2)
        zT = view(prep, 9216, 4, SEQ - CHUNK)
        tt, ttT, loT, xx, rhs, wu = (view(prep, i * 512, 4, P) for i in range(6))
        toks = view(un, 0, 4, 512)
        v0n = view(un, 2048, H, P)
        stn = view(un, 3072, 4, HD)
        st = view(un, 3328, NCH - 1, 4, HD)
        gT = view(un, 4096, NCH - 2, 4, HD)
        lakT, mrkT, lbT, mrbT = (view(un, 4608 + i * 512, 4, P) for i in range(4))
        hP = proj[:, T_R:T_R + 3, :].rearrange("p a t -> p (a t)")[:, 0:768].rearrange("p (q m c) -> p q m c", q=NCH - 1, m=4)
        qh = un[0:96, 0:2048].rearrange("p (h t) -> p h t", h=H)
        kh = un[0:96, 2048:4096].rearrange("p (h t) -> p h t", h=H)
        fa = un[96:98, 0:2048].rearrange("p (h t) -> p h t", h=H)
        fb = un[96:98, 2048:4096].rearrange("p (h t) -> p h t", h=H)
        vm = view(un, 4096, TB, 512)
        sc, pp, pT = (view(un, 5120 + i * 768, 2, 384) for i in range(3))
        rtmp = un[64:96, 5120:7168].rearrange("p (h t) -> p h t", h=H)
        flog, ft, fcum, fneg = (un[0:8, 8192 + i * 256:8448 + i * 256] for i in range(4))
        lat = view(un, 1024, 4, SEQ)
        gate = view(un, 8704, 2, SEQ)
        gr = view(un, 0, KT, SEQ)
        merged = view(un, 6656, KT, SEQ)
        cg = un[:, 6144:8192].rearrange("p (j e t) -> p j e t", j=4, e=2)
        sg = view(un, 8192, 4, SEQ)

        ps = ctx.enter_context(nc.psum_tensor("ps", [P, 8, 512], F32))

        def done(l, u):
            return l * N_UNITS + u + 1 + RING

        def a_at(l, u):
            return l * N_A + A_PLACE[u] + RING

        def v_at(l, u):
            return l * N_V + V_PLACE[u]

        def mm_at(l, name):
            return l * N_MM + RK_MM[name]

        def ev_at(l, name):
            return l * N_EV + RK_EV[name]

        def two(bank):
            return ps[:, bank, :].rearrange("p (a t) -> p a t", a=2)

        def four(bank):
            return ps[:, bank, :].rearrange("p (a t) -> p a t", a=4)

        def span(bank):
            return ps[:, bank:bank + 2, :].rearrange("p b (a t) -> p (b a) t", a=2)

        landed = [sem(f"landed{s}") for s in range(RING)]
        hi_ok, lo_ok, unit_done = sem("hi_ok"), sem("lo_ok"), sem("unit_done")
        a_free, v_free = sem("a_free"), sem("v_free")
        loaded = sem("loaded")
        ada_first = [sem("ada_first0"), sem("ada_first1")]
        ada_in, ada_used, mod_ps, mod_ok = sem("ada_in"), sem("ada_used"), sem("mod_ps"), sem("mod_ok")
        trig_r, trig_ok, csig_ok = sem("trig_r"), sem("trig_ok"), sem("csig_ok")
        dv, passed = sem("dv"), sem("passed")
        sq_ok, ss_ps, rec_ok, rt_ok = sem("sq_ok"), sem("ss_ps"), sem("rec_ok"), sem("rt_ok")
        t_norm, hh_ok, h_ok = sem("t_norm"), sem("hh_ok"), sem("h_ok")
        in_ok, sh_ok, sl_ok = sem("in_ok"), sem("sh_ok"), sem("sl_ok")
        shift_ok, lora_ev, kq_ok, fac_ok = sem("shift_ok"), sem("lora_ev"), sem("kq_ok"), sem("fac_ok")
        cum_ok, exp_ok = sem("cum_ok"), sem("exp_ok")
        rk_mm, rk_ev, t_ok = sem("rk_mm"), sem("rk_ev"), sem("t_ok")
        up_ok, rope_ok = sem("up_ok"), sem("rope_ok")
        fl_in, fl_exp, fl_cum, fl_dma = sem("fl_in"), sem("fl_exp"), sem("fl_cum"), sem("fl_dma")
        s_ps, s_ok, p_ok, pn_ok = sem("s_ps"), sem("s_ok"), sem("p_ok"), sem("pn_ok")
        pt_ps, pt_ok, o_ps, o_ok = sem("pt_ps"), sem("pt_ok"), sem("o_ps"), sem("o_ok")
        mg_ok, x_ok = sem("mg_ok"), sem("x_ok")
        cv_ok, cv2_ok, taps_ok, si_ok = sem("cv_ok"), sem("cv2_ok"), sem("taps_ok"), sem("si_ok")
        mul_ok, ah_ok, act_ok, dn_ps = sem("mul_ok"), sem("ah_ok"), sem("act_ok"), sem("dn_ps")
        fin_ok, out_ok = sem("fin_ok"), sem("out_ok")

        ident = cn[:, K_ID:K_ID + P]
        ones = cn[:, K_ONES:K_ONES + P]
        blk = cn[:, K_BLK:K_BLK + P]
        LV = len(LEVELS)
        GROUPS = [(b, par_) for b in range(TB) for par_ in range(2)]

        def alone(eng):
            eng.sem_inc(passed, 1)

        block = ctx.enter_context(nc.Block())

        @block.sync
        def _(sp):
            def load(n, s):
                sp.wait_ge(lo_ok, n + 1)
                sp.dma_start(raw[:, s, :], ws[bass.ds(n, 1), :, :].rearrange("a p n -> (a p) n")).then_inc(landed[s], 16)

            for dst, src in ((cn[:, :], con), (parall[:, :, :], par), (cc[:, :], cT), (x[:, :, :], xT),
                             (posi[:, :], pos)):
                sp.dma_start(dst, src).then_inc(loaded, 16)
            with sp.Fori(0, (DEPTH * N_UNITS + AHEAD) // RING) as i:
                for s in range(RING):
                    load(i * RING + s, s)
            for n in range((DEPTH * N_UNITS + AHEAD) // RING * RING, DEPTH * N_UNITS + AHEAD):
                load(n, n % RING)
            sp.wait_ge(fin_ok, 1)
            sp.dma_start(out, sq).then_inc(out_ok, 16)
            sp.wait_ge(out_ok, 16)

        @block.gpsimd
        def _(pool):
            def piece(t, k, slot, free, signal=ada_in):
                pool.wait_ge(ada_used, free)
                alone(pool)
                pool.dma_start(ada[slot], wada[bass.ds(t * KT + k, 1), :, :].rearrange("a p n -> (a p) n")
                               ).then_inc(signal, 16)

            for k in range(KT):
                piece(0, k, k % 2, k + 1, ada_first[k % 2])
            with pool.Fori(0, DEPTH) as l:
                for k in range(KT):
                    piece(l * 3 + 1, k, 0, l * 24 + 8 + k + 2)
                pool.wait_ge(fl_cum, l + 1)
                alone(pool)
                pool.dma_start(fa[0:1, :, :].rearrange("p h t -> p (h t)"), fcum).then_inc(fl_dma, 16)
                pool.dma_start(fb[1:2, :, :].rearrange("p h t -> p (h t)"), fneg).then_inc(fl_dma, 16)
                pool.wait_ge(rk_mm, mm_at(l, "y"))
                for j in (2, 3):
                    for k in range(KT):
                        piece(l * 3 + j, k, 0, l * 24 + j * 8 + k + 2)

        @block.scalar
        def _(a):
            def hi(l, u):
                a.wait_ge(landed[u % RING], (l * (N_UNITS // RING) + u // RING + 1) * 16)
                a.wait_ge(unit_done, l * N_UNITS + u + 1)
                a.activation(wh[:, u % RING, :], raw[:, u % RING, :], ACT.Copy).then_inc(hi_ok, 1)

            def split(nth, dst, src):
                a.wait_ge(in_ok, nth)
                a.activation(dst, src, ACT.Copy).then_inc(sh_ok, 1)

            a.wait_ge(loaded, 16 * 5)
            a.activation(csig[:, :], cc[:, :], ACT.Sigmoid).then_inc(csig_ok, 1)
            a.wait_ge(trig_r, 1)
            a.activation(trig[:, :], trig[:, :], ACT.Sin).then_inc(trig_ok, 1)
            for u in range(AHEAD):
                hi(0, u)
            with a.Fori(0, DEPTH) as l:
                def root(nth, n):
                    a.wait_ge(rec_ok, l * N_NORM + nth)
                    a.activation(rs[:, 0:n, :], rs[:, 0:n, :], ACT.Sqrt).then_inc(rt_ok, 1)

                def norm(nth, h0, sh_col):
                    root(nth, 1)
                    for k in range(KT):
                        a.wait_ge(t_norm, l * 2 * KT + (h0 > 0) * KT + k + 1)
                        a.activation(hh[:, k, :], sq[:, k, :], ACT.Identity, bias=mod[:, sh_col + k:sh_col + k + 1]
                                     ).then_inc(hh_ok, 1)

                def project(u):
                    a.wait_ge(unit_done, done(l, u))
                    a.activation(proj[:, u if u < U_LORA else u - 2, 1:SEQ + 1], ps[:, u % RING, 0:SEQ], ACT.Copy).then_inc(a_free, 1)

                norm(1, H_N1, 0)
                with a.Fori(0, 5) as i:
                    for s in range(RING):
                        a.wait_ge(landed[(s + 2) % RING], (l * (N_UNITS // RING) + i + (s + 2) // RING + 1) * 16)
                        a.wait_ge(unit_done, l * N_UNITS + i * RING + s + 3)
                        a.activation(wh[:, (s + 2) % RING, :], raw[:, (s + 2) % RING, :], ACT.Copy).then_inc(hi_ok, 1)
                        a.wait_ge(unit_done, done(l, i * RING + s))
                        a.activation(proj[:, bass.ds(i * RING + s, 1), 1:SEQ + 1], ps[:, s, 0:SEQ], ACT.Copy).then_inc(a_free, 1)
                hi(l, 17)
                a.wait_ge(shift_ok, l * 5 + 1)
                a.activation(tw[0:64, 0, :], proj[0:64, T_WA, 1:], ACT.Tanh)
                a.activation(tw[64:128, 0, :], proj[64:128, T_WA, 1:], ACT.Copy)
                a.activation(tw[:, 1, :], proj[:, T_GL, 1:], ACT.Sigmoid).then_inc(in_ok, 1)
                split(l * 3 + 1, sh[:, 0:2, :], tw)
                a.activation(sh[:, 2, :], proj[:, T_MIX, 1:], ACT.Copy).then_inc(sh_ok, 1)
                project(15)
                hi(l, 18)
                project(16)
                a.wait_ge(shift_ok, l * 5 + 5)
                for m in range(4):
                    a.activation(kkn[:, m, :], proj[:, T_K + m, 1:], ACT.Copy, scale=pr[:, C_KK + m:C_KK + m + 1])
                for m in range(4):
                    last = a.activation(sqk[:, m, :], proj[:, T_K + m, 1:], ACT.Square, scale=pr[:, C_KK + m:C_KK + m + 1])
                last.then_inc(kq_ok, 1)
                for u in (17, 18):
                    hi(l, u + 2)
                    project(u)
                hi(l, 21)
                a.wait_ge(unit_done, done(l, U_LORA))
                for m in range(4):
                    a.activation(lgd[:, m, :], span(3)[:, m, :], ACT.Sigmoid, bias=pr[:, C_W0 + m:C_W0 + m + 1]).then_inc(lora_ev, 1)
                a.activation(gg[:, 2:4, :], two(U_LORA % RING), ACT.Copy).then_inc(a_free, 1)
                hi(l, 22)
                for m in range(4):
                    a.activation(aa[:, m, :], span(5)[:, m, :], ACT.Sigmoid, bias=pr[:, C_A0 + m:C_A0 + m + 1]).then_inc(lora_ev, 1)
                a.activation(gg[:, 0:2, :], two(7), ACT.Copy).then_inc(lora_ev, 1)
                a.wait_ge(unit_done, done(l, U_LORA + 1))
                for m in range(2):
                    last = a.activation(tmp[:, m, :], two((U_LORA + 1) % RING)[:, m, :], ACT.Sigmoid, bias=pr[:, C_V0 + m:C_V0 + m + 1])
                last.then_inc(a_free, 1)
                for m in range(2, 4):
                    last = a.activation(tmp[:, m, :], two(3)[:, m - 2, :], ACT.Sigmoid, bias=pr[:, C_V0 + m:C_V0 + m + 1])
                last.then_inc(lora_ev, 1)
                a.wait_ge(lora_ev, l * 10 + 8)
                for m in range(4):
                    last = a.activation(fac[:, m, :], aa[:, m, :], ACT.Identity, bias=ka1[:, m:m + 1], scale=pr[:, C_KA + m:C_KA + m + 1])
                last.then_inc(fac_ok, 1)
                hi(l, 23)
                project(21)
                a.wait_ge(cum_ok, l * 2 + 1)
                a.activation(ar[:, :, :, 1, :], cum.rearrange("p m (b t) -> p m b t", b=TB), ACT.Exp, scale=-RSQ_E)
                a.activation(kap, cum, ACT.Exp, scale=RSQ_E)
                hi(l, 24)
                project(22)
                a.activation(ar[:, :, :, 0, :], lgd.rearrange("p m (b t) -> p m b t", b=TB), ACT.Exp, scale=-RSQ_E).then_inc(exp_ok, 1)
                hi(l, 25)
                project(23)
                hi(l, 26)
                project(24)
                root(2, 2)
                hi(l, 27)
                project(25)
                a.wait_ge(cum_ok, l * 2 + 2)
                a.activation(tmp, tmp, ACT.Sqrt).then_inc(exp_ok, 1)
                split(l * 3 + 2, sh[:, :, :], lat)
                for u in (26, 27, 28):
                    hi(l, u + 2)
                    project(u)
                for e in range(2):
                    hi(l, 31 + 2 * e)
                    a.wait_ge(unit_done, done(l, U_FV + 2 * e + 1))
                    a.activation(vf[:, :, e * 256:(e + 1) * 256], two((U_FV + 2 * e + 1) % RING), ACT.Copy).then_inc(a_free, 1)
                    hi(l, 32 + 2 * e)
                a.wait_ge(fl_in, l + 1)
                a.activation(ft, ft, ACT.Exp).then_inc(fl_exp, 1)
                a.wait_ge(fl_exp, l * 2 + 1)
                a.activation(ft, ft, ACT.Ln, bias=1.0).then_inc(fl_exp, 1)
                for e in range(2):
                    hi(l, 35 + e)
                    a.wait_ge(unit_done, done(l, U_QUP + e))
                    a.activation(qh[0:64, 4 * e:4 * e + 4, :], span(5 - 2 * e)[0:64], ACT.Copy).then_inc(up_ok, 1)
                hi(l, 37)
                a.wait_ge(unit_done, done(l, U_KUP))
                kk = kh.rearrange("p (m e) t -> p m e t", e=2)
                for e in range(2):
                    a.activation(kk[0:64, :, e, :], span(5)[64 * e:64 * e + 64], ACT.Copy).then_inc(up_ok, 1)
                hi(l, 38)
                a.wait_ge(unit_done, done(l, U_VUP))
                a.activation(vm, ps[:, 3:5, :], ACT.Copy).then_inc(up_ok, 1)
                for n in range(2 * H):
                    scale = HD ** -0.5 if n < H else (NOPE + ROPE) ** -0.5
                    a.wait_ge(s_ok, l * 2 * H + n + 1)
                    if n >= 2:
                        a.wait_ge(pt_ps, l * 2 * H + n - 1)
                    a.activation(pp[:, n % 2, 0:128], sc[:, n % 2, 0:128], ACT.Exp, bias=nb[:, n % 2, 0:1],
                                 scale=scale, accum_out=den[:, n % 2, 0:1])
                    a.activation(pp[:, n % 2, 128:384], sc[:, n % 2, 128:384], ACT.Exp, bias=nb[:, n % 2, 1:2],
                                 scale=scale, accum_out=den[:, n % 2, 1:2]).then_inc(p_ok, 1)
                    a.wait_ge(pt_ps, l * 2 * H + n + 1)
                    if n >= 2:
                        a.wait_ge(o_ps, l * 2 * H + n - 1)
                    a.activation(pT[:, n % 2, :], ps[:, 2 + n % 2, 0:384], ACT.Copy).then_inc(pt_ok, 1)
                    if n % 2:
                        a.wait_ge(o_ps, l * 2 * H + n + 1)
                        a.activation(y[:, 4 + n // 2, :], ps[:, 4 + n // 2 % 2, 0:SEQ], ACT.Copy).then_inc(o_ok, 1)
                a.wait_ge(o_ok, l * H + H)

                def gated(u, dst):
                    a.wait_ge(unit_done, done(l, u))
                    a.activation(dst, ps[:, u % RING, 0:SEQ], ACT.Sigmoid).then_inc(a_free, 1)

                for g, (b, par_) in enumerate(GROUPS):
                    u0 = U_GB + 6 * g

                    def gb(u):
                        e = (u - U_GB) % 3
                        if e < 2:
                            if u >= U_GB + 3:
                                a.wait_ge(v_free, v_at(l, u - e - 1))
                            gated(u, gate[:, e, :])

                    if g % 2 == 0:
                        a.wait_ge(unit_done, done(l, u0 - 1))
                        a.activation(sh[:, :, :], y[:, 4 + 2 * g:8 + 2 * g, :], ACT.Copy).then_inc(sh_ok, 1)
                    hi(l, u0 + 2)
                    gb(u0)
                    for i in range(LV):
                        a.wait_ge(rk_mm, mm_at(l, f"X{b}{par_}{i}"))
                        a.activation(xx, four(3), ACT.Copy).then_inc(rk_ev, 1)
                        hi(l, u0 + i + 3)
                        gb(u0 + i + 1)
                    a.wait_ge(rk_mm, mm_at(l, f"WU{b}{par_}"))
                    a.activation(wu, four(7), ACT.Copy).then_inc(rk_ev, 1)
                for t in range(KT):
                    hi(l, U_GR + t + 2)
                    gated(U_GR + t, gr[:, t, :])
                    if t == 5:
                        a.wait_ge(rk_ev, ev_at(l, "var"))
                        a.activation(tmp, tmp, ACT.Sqrt).then_inc(exp_ok, 1)
                split(l * 3 + 3, sh[:, :, :], y[:, 0:4, :])
                for i in range(4):
                    hi(l, U_BR + i + 2)
                    a.wait_ge(mg_ok, l * 4 + i + 1)
                    a.activation(hh[:, 2 * i:2 * i + 2, :], merged[:, 2 * i:2 * i + 2, :], ACT.Copy).then_inc(hh_ok, 1)
                for t in range(KT):
                    hi(l, U_WO + t + 2)
                norm(3, H_N2, 24)

                def conv(j, r):
                    a.wait_ge(unit_done, l * N_UNITS + RING + (up_unit(j) if isinstance(j, int) else U_FF + 4 + 3 * (j - 2)) + 2)
                    for e in range(2):
                        last = a.activation(cg[:, r, e, :], two(r)[:, e, :], ACT.Identity,
                                            bias=pr[:, bass.ds(C_CB + e * FT + j, 1)], scale=pr[:, bass.ds(C_CW + (4 + e) * FT + j, 1)])
                    last.then_inc(cv_ok, 1)

                def silu(j, r):
                    a.wait_ge(cv2_ok, l * FT + j + 1)
                    a.activation(sg[:, r, :], cg[:, r, 0, :], ACT.Silu).then_inc(si_ok, 1)

                def act_hi(j, r):
                    a.wait_ge(mul_ok, l * FT + j + 1)
                    a.activation(sh[:, r, :], sg[:, r, :], ACT.Copy).then_inc(ah_ok, 1)

                for j in range(2):
                    hi(l, U_FF + 2 * j + 2)
                    hi(l, U_FF + 2 * j + 3)
                    if j:
                        act_hi(0, 0)
                    conv(j, j)
                    silu(j, j)
                with a.Fori(0, (FT - 2) // 4) as i:
                    for o in range(4):
                        j, r = 2 + 4 * i + o, (2 + o) % 4

                        def hi_ff(e):
                            s = (U_FF + 3 * o + e) % RING
                            a.wait_ge(landed[s], (l * (N_UNITS // RING) + i * 4 + (U_FF + 6 + 3 * o + e) // RING + 1) * 16)
                            a.wait_ge(unit_done, l * N_UNITS + i * 12 + U_FF + 6 + 3 * o + e + 1)
                            a.activation(wh[:, s, :], raw[:, s, :], ACT.Copy).then_inc(hi_ok, 1)

                        hi_ff(0)
                        hi_ff(1)
                        act_hi(j - 1, (r + 3) % 4)
                        conv(j, r)
                        hi_ff(2)
                        silu(j, r)
                act_hi(FT - 1, (FT - 1) % 4)
                hi(l, N_UNITS)
                hi(l, N_UNITS + 1)
            a.wait_ge(rec_ok, DEPTH * N_NORM + 1)
            a.activation(rs[:, 0:1, :], rs[:, 0:1, :], ACT.Sqrt).then_inc(rt_ok, 1)

        @block.vector
        def _(v):
            count = [0]
            base = [0]

            def step(ins):
                ins.then_inc(dv, 1)
                count[0] += 1
                v.wait_ge(dv, base[0] + count[0])

            def lo(l, u):
                v.wait_ge(hi_ok, l * N_UNITS + u + 1)
                v.tensor_tensor(wl[:, u % RING, :], raw[:, u % RING, :], wh[:, u % RING, :], ALU.subtract).then_inc(lo_ok, 1)

            def piece(t, k, slot=0, first=None):
                if isinstance(t, int):
                    v.wait_ge(ada_first[slot], (k // 2 + 1) * 16)
                else:
                    v.wait_ge(ada_in, ((t - 1) * KT + k + 1) * 16)
                if first if first is not None else (isinstance(k, int) and k == 0):
                    if not (isinstance(t, int) and t == 0):
                        v.wait_ge(mod_ps, t)
                    v.tensor_scalar(acc, ada[slot], cc[:, 0:1], None, ALU.mult).then_inc(ada_used, 1)
                else:
                    v.wait_ge(ada_used, t * KT + k + 2)
                    v.scalar_tensor_tensor(acc, ada[slot], cc[:, bass.ds(k, 1)] if not isinstance(k, int) else cc[:, k:k + 1], acc,
                                           ALU.mult, ALU.add).then_inc(ada_used, 1)

            def mod_third(t, bank, dst, bias):
                v.wait_ge(mod_ps, t + 1)
                v.tensor_tensor(dst, ps[:, bank, 0:16], bias, ALU.add).then_inc(mod_ok, 1)
                v.wait_ge(mod_ok, t + 1)

            def inv_square(nth, bank, n, width):
                v.wait_ge(ss_ps, nth)
                step(v.tensor_scalar(rs[:, 0:n, :], two(bank)[:, 0:n, :], 1.0 / width, 1e-6, ALU.mult, ALU.add))
                v.reciprocal(rs[:, 0:n, :], rs[:, 0:n, :]).then_inc(rec_ok, 1)
                v.wait_ge(rt_ok, nth)

            v.sem_inc(unit_done, RING)
            v.sem_inc(lo_ok, RING)
            v.sem_inc(a_free, RING)
            v.sem_inc(ada_used, 2)
            v.sem_inc(taps_ok, 4)
            v.memset(v1st[:, :, :], 0.0)
            v.memset(proj[:, :, 0:1], 0.0)
            v.wait_ge(loaded, 16 * 5)
            v.wait_ge(csig_ok, 1)
            step(v.tensor_tensor(cc[:, :], cc[:, :], csig[:, :], ALU.mult))
            step(v.tensor_copy(sq[:, 0, :], posi[:, :]))
            step(v.tensor_scalar(sq[:, 0, :], sq[:, 0, :], cn[:, K_TRIG:K_TRIG + 1], None, ALU.mult))
            step(v.tensor_scalar(sq[:, 1, :], sq[:, 0, :], 1.0 / TWO_PI, cn[:, K_TRIG + 1:K_TRIG + 2], ALU.mult, ALU.add))
            step(v.tensor_scalar(sq[:, 2, :], sq[:, 1, :], MAGIC, None, ALU.add))
            step(v.tensor_scalar(sq[:, 1, :], sq[:, 2, :], MAGIC, None, ALU.subtract))
            for c in (PI2_A, PI2_B, PI2_C):
                step(v.scalar_tensor_tensor(sq[:, 0, :], sq[:, 1, :], -c, sq[:, 0, :], ALU.mult, ALU.add))
            step(v.tensor_scalar(sq[:, 0, :], sq[:, 0, :], cn[:, K_TRIG + 2:K_TRIG + 3], None, ALU.add))
            v.tensor_scalar(trig[:, :], sq[:, 0, :], -3.1415925, 3.1415925, ALU.max, ALU.min).then_inc(trig_r, 1)
            v.wait_ge(trig_ok, 1)
            step(v.tensor_scalar(trig[:, :], trig[:, :], cn[:, K_TRIG + 3:K_TRIG + 4], None, ALU.mult))
            for k in range(KT):
                piece(0, k, k % 2)
            for u in range(AHEAD):
                lo(0, u)
            mod_third(0, 3, mod[:, 0:16], parall[:, 0, C_BADA:C_BADA + 16])
            pre = count[0]
            count[0] = 0

            with v.Fori(0, DEPTH) as l:
                base[0] = l * N_DV + pre
                step(v.tensor_copy(pr[:, :], parall[:, bass.ds(l, 1), :]))
                v.tensor_scalar(ka1[:, :], pr[:, C_KA:C_KA + 4], -1.0, 1.0, ALU.mult, ALU.add)

                def norm(nth, g_col, sc_col, sh_col, h0):
                    v.tensor_scalar(gain[:, :], mod[:, sc_col:sc_col + KT], 1.0, None, ALU.add)
                    v.tensor_tensor(sq, x[:, :, :], x[:, :, :], ALU.mult).then_inc(sq_ok, 1)
                    v.wait_ge(sq_ok, l * N_NORM + nth)
                    step(v.tensor_tensor(gain[:, :], gain[:, :], pr[:, g_col:g_col + KT], ALU.mult))
                    inv_square(l * N_NORM + nth, 3, 1, D_MODEL)
                    for k in range(KT):
                        v.scalar_tensor_tensor(sq[:, k, :], x[:, k, :], gain[:, k:k + 1], rs[:, 0, :], ALU.mult, ALU.mult
                                               ).then_inc(t_norm, 1)
                    for k in range(KT):
                        v.wait_ge(hh_ok, l * N_H + h0 + k + 1)
                        v.scalar_tensor_tensor(hl[:, k, :], sq[:, k, :], mod[:, sh_col + k:sh_col + k + 1], hh[:, k, :],
                                               ALU.add, ALU.subtract).then_inc(h_ok, 1)

                def sub_split(n, dst, src, leading):
                    v.wait_ge(sh_ok, n)
                    v.tensor_tensor(dst, src, leading, ALU.subtract).then_inc(sl_ok, 1)

                norm(1, C_N1, 8, 0, H_N1)
                piece(l * 3 + 1, 0)

                per = 1
                outer = base[0]
                with v.Fori(0, 5) as i:
                    base[0] = outer + i * per
                    start = count[0]
                    for s in range(RING):
                        t = (s + 2) % RING
                        v.wait_ge(hi_ok, l * N_UNITS + i * RING + s + 3)
                        v.tensor_tensor(wl[:, t, :], raw[:, t, :], wh[:, t, :], ALU.subtract).then_inc(lo_ok, 1)
                    piece(l * 3 + 1, i + 1, first=False)
                    v.wait_ge(a_free, l * N_A + i * RING + 3 + RING)
                    step(v.tensor_tensor(shd, proj[:, bass.ds(i * 3, 3), 0:SEQ], proj[:, bass.ds(i * 3, 3), 1:SEQ + 1], ALU.subtract))
                    for t in range(3):
                        ins = v.scalar_tensor_tensor(proj[:, bass.ds(i * 3 + t, 1), 1:SEQ + 1], shd[:, t:t + 1, :],
                                                     pr[:, bass.ds(C_MU + i * 3 + t, 1)],
                                                     proj[:, bass.ds(i * 3 + t, 1), 1:SEQ + 1], ALU.mult, ALU.add)
                    ins.then_inc(shift_ok, 1)
                    assert count[0] - start == per
                base[0] = outer
                count[0] += 4 * per
                rr, kx, vx = (proj[:, t:t + 4, 1:SEQ + 1] for t in (T_R, T_K, T_V))
                lo(l, 17)
                v.wait_ge(sh_ok, l * (N_SPLIT + 1) + 2)
                v.tensor_tensor(sl[:, 0:2, :], tw, sh[:, 0:2, :], ALU.subtract)
                v.tensor_tensor(sl[:, 2, :], proj[:, T_MIX, 1:], sh[:, 2, :], ALU.subtract).then_inc(sl_ok, 1)
                lo(l, 18)
                piece(l * 3 + 1, 6)
                lo(l, 19)
                piece(l * 3 + 1, 7)
                lo(l, 20)
                v.wait_ge(a_free, a_at(l, 18))
                v.tensor_tensor(sq[:, 0:4, :], proj[:, T_MQ:T_MQ + 4, 1:], proj[:, T_MQ:T_MQ + 4, 1:], ALU.mult).then_inc(sq_ok, 1)
                lo(l, 21)
                lo(l, 22)
                for m in range(4):
                    v.wait_ge(lora_ev, l * 10 + m + 1)
                    ins = v.tensor_tensor_scan(cum[:, m, :], cn[:, K_RST:K_RST + SEQ], lgd[:, m, :], 0.0, ALU.mult, ALU.add)
                step(ins)
                v.tensor_tensor(lgd, cum, lgd, ALU.subtract).then_inc(cum_ok, 1)
                lo(l, 23)
                step(v.tensor_tensor(vt, v1st[:, :, :], vx, ALU.subtract))
                v.wait_ge(lora_ev, l * 10 + 10)
                step(v.scalar_tensor_tensor(vt, vt, pr[:, C_FLAG:C_FLAG + 1], tmp, ALU.mult, ALU.mult))
                step(v.tensor_tensor(vx, vx, vt, ALU.add))
                lo(l, 24)
                v.scalar_tensor_tensor(v1st[:, :, :], vx, pr[:, C_FLAG + 1:C_FLAG + 2], v1st[:, :, :], ALU.mult, ALU.add)
                v.wait_ge(fac_ok, l + 1)
                step(v.tensor_tensor(kx, kx, fac, ALU.mult))
                v.wait_ge(exp_ok, l * 3 + 1)
                for m in range(4):
                    ins = v.scalar_tensor_tensor(bon[:, m, :], rr[:, m, :], pr[:, C_RK + m:C_RK + m + 1], kx[:, m, :], ALU.mult, ALU.mult)
                ins.then_inc(rk_ev, 1)
                lo(l, 25)
                v.wait_ge(rk_mm, mm_at(l, "ksq"))
                step(v.tensor_scalar(tmp, span(5), 1e-24, None, ALU.max))
                v.reciprocal(tmp, tmp).then_inc(cum_ok, 1)
                lo(l, 26)
                inv_square(l * N_NORM + 2, 7, 2, 256)
                for t in range(4):
                    ins = v.scalar_tensor_tensor(lat[:, t, :], proj[:, T_MQ + t, 1:], pr[:, C_MQ + t:C_MQ + t + 1], rs[:, t // 2, :],
                                                 ALU.mult, ALU.mult)
                ins.then_inc(in_ok, 1)
                lo(l, 27)
                mod_third(l * 3 + 1, 7, mod[:, 16:32], pr[:, C_BADA + 16:C_BADA + 32])
                for b in range(TB):
                    v.tensor_copy(pc[:, :, 2 * b:2 * b + 2], ar[:, :, b, 1, :].rearrange("p m (c t) -> p m c t", c=2)[:, :, :, CHUNK - 1])
                v.wait_ge(rk_mm, mm_at(l, "bonus"))
                v.tensor_tensor(bon, span(3), vx, ALU.mult).then_inc(rk_ev, 1)
                lo(l, 28)
                sub_split(l * (N_SPLIT + 1) + 3, sl[:, :, :], lat, sh[:, :, :])
                v.wait_ge(exp_ok, l * 3 + 2)
                step(v.tensor_tensor(kkn, kkn, tmp, ALU.mult))
                lo(l, 29)
                step(v.tensor_tensor(bet, kkn, aa, ALU.mult))
                v.tensor_tensor(bet, bet, kap, ALU.mult)
                step(v.tensor_tensor(kap, kx, kap, ALU.mult))
                lo(l, 30)
                v.tensor_tensor(ar[:, :, :, 0, :], ar[:, :, :, 0, :], kkn.rearrange("p m (b t) -> p m b t", b=TB), ALU.mult)
                step(v.tensor_scalar(flog, proj[0:8, T_MIX, 1:SEQ + 1], pr[0:8, C_MIX:C_MIX + 1], None, ALU.add))
                step(v.tensor_scalar(fneg, flog, -1.0, None, ALU.mult))
                v.tensor_tensor(ft, flog, fneg, ALU.min).then_inc(fl_in, 1)
                v.wait_ge(fl_in, l + 1)
                step(v.tensor_scalar(flog, flog, 0.0, None, ALU.min))
                lo(l, 31)
                lo(l, 32)
                v.tensor_tensor(ar[:, :, :, 1, :], ar[:, :, :, 1, :], rr.rearrange("p m (b t) -> p m b t", b=TB), ALU.mult
                                ).then_inc(rk_ev, 1)
                v.wait_ge(rk_ev, ev_at(l, "rho"))
                lo(l, 33)
                cos = trig[64:96, :].rearrange("p (a t) -> p a t", a=1)
                sin = trig[96:128, :].rearrange("p (a t) -> p a t", a=1)
                v.tensor_tensor(rtmp[:, 0, :], proj[96:128, T_MIX, 1:SEQ + 1], trig[96:128, :], ALU.mult)
                step(v.tensor_tensor(rtmp[:, 1, :], proj[64:96, T_MIX, 1:SEQ + 1], trig[64:96, :], ALU.mult))
                step(v.tensor_tensor(rtmp[:, 0, :], rtmp[:, 0, :], rtmp[:, 1, :], ALU.add))
                step(v.tensor_copy(kh[64:96, :, :], rtmp[:, 0:1, :].broadcast_to([32, H, SEQ])))
                lo(l, 34)
                v.wait_ge(fl_exp, l * 2 + 2)
                step(v.tensor_tensor(flog, flog, ft, ALU.subtract))
                step(v.tensor_tensor_scan(ft, cn[0:8, K_ONES:K_ONES + SEQ], flog, 0.0, ALU.mult, ALU.add))
                v.tensor_scalar(fcum, ft, 8.0, None, ALU.mult)
                v.memset(fa[:, :, :], 1.0)
                v.memset(fb[:, :, :], 1.0)
                v.tensor_scalar(fneg, ft, -8.0, None, ALU.mult).then_inc(fl_cum, 1)
                for e in range(2):
                    lo(l, 35 + e)
                    v.wait_ge(up_ok, l * 5 + e + 1)
                    o = span(5 - 2 * e)
                    v.tensor_tensor(rtmp[:, 4 * e:4 * e + 4, :], o[96:128], sin.broadcast_to([32, 4, SEQ]), ALU.mult)
                    step(v.tensor_tensor(qh[64:96, 4 * e:4 * e + 4, :], o[64:96], cos.broadcast_to([32, 4, SEQ]), ALU.mult))
                    v.tensor_tensor(qh[64:96, 4 * e:4 * e + 4, :], qh[64:96, 4 * e:4 * e + 4, :], rtmp[:, 4 * e:4 * e + 4, :],
                                    ALU.add).then_inc(rope_ok, 1)
                lo(l, 37)
                lo(l, 38)

                for n in range(2 * H):
                    scale = HD ** -0.5 if n < H else (NOPE + ROPE) ** -0.5
                    v.wait_ge(s_ps, l * 2 * H + n + 1)
                    if n >= 2:
                        v.wait_ge(p_ok, l * 2 * H + n - 1)
                    alone(v)
                    v.tensor_tensor_reduce(sc[:, n % 2, 0:128], ps[:, n % 2, 0:128], cn[:, K_CAUS + 128:K_CAUS + 256],
                                           1.0, NEG, ALU.add, ALU.max, mx[:, n % 2, 0:1])
                    step(v.tensor_tensor_reduce(sc[:, n % 2, 128:384], ps[:, n % 2, 128:384], cn[:, K_CAUS:K_CAUS + 256],
                                                1.0, NEG, ALU.add, ALU.max, mx[:, n % 2, 1:2]))
                    v.tensor_scalar(nb[:, n % 2, :], mx[:, n % 2, :], -scale, None, ALU.mult).then_inc(s_ok, 1)
                    v.wait_ge(p_ok, l * 2 * H + n + 1)
                    step(v.reciprocal(rd[:, n % 2, :], den[:, n % 2, :]))
                    v.tensor_scalar(pp[:, n % 2, 0:128], pp[:, n % 2, 0:128], rd[:, n % 2, 0:1], None, ALU.mult)
                    v.tensor_scalar(pp[:, n % 2, 128:384], pp[:, n % 2, 128:384], rd[:, n % 2, 1:2], None,
                                    ALU.mult).then_inc(pn_ok, 1)

                def evac(ins, name):
                    ins.then_inc(rk_ev, 1)
                    v.wait_ge(rk_ev, ev_at(l, name))

                def mask(at, n=4):
                    return cn[:, at:at + P].rearrange("p (a t) -> p a t", a=1).broadcast_to([P, n, P])

                def merge(u, tiles, gates, first):
                    v.wait_ge(unit_done, done(l, u))
                    src = two(u % RING)
                    if first:
                        v.tensor_tensor(merged[:, tiles, :], src, gates, ALU.mult).then_inc(v_free, 1)
                    else:
                        step(v.tensor_tensor(gates, src, gates, ALU.mult))
                        v.tensor_tensor(merged[:, tiles, :], merged[:, tiles, :], gates, ALU.add).then_inc(v_free, 1)

                def merge_gb(u):
                    i = (u - U_GB) // 3 % 4
                    v.wait_ge(a_free, a_at(l, u - 1))
                    if u >= U_GB + 12:
                        v.wait_ge(v_free, v_at(l, u - 3))
                    merge(u, slice(2 * i, 2 * i + 2), gate, u < U_GB + 12)

                for g, (b, par_) in enumerate(GROUPS):
                    u0 = U_GB + 6 * g
                    name = f"{b}{par_}"
                    if g % 2 == 0:
                        sub_split(l * (N_SPLIT + 1) + 4 + g // 2, sl[:, :, :], y[:, 4 + 2 * g:8 + 2 * g, :], sh[:, :, :])
                        v.wait_ge(rk_mm, mm_at(l, f"tr{b}"))
                        for i in range(4):
                            v.tensor_copy(toks[:, i, :], ps[:, 3 + i, :])
                        if b == 0:
                            v.memset(v0n[:, :, 0:64], 0.0)
                        evac(v.tensor_scalar(v0n[:, :, 64:128], ps[:, 6, :].rearrange("p (h c) -> p h c", h=H), -1.0, None, ALU.mult),
                             f"tr{b}")
                    lo(l, u0 + 2)
                    v.wait_ge(rk_mm, mm_at(l, f"S{name}"))
                    v.tensor_tensor(lakT, span(3)[:, :, 0:128], mask(K_MS), ALU.mult)
                    step(v.tensor_tensor(lbT, span(5)[:, :, 0:128], mask(K_MS), ALU.mult))
                    v.tensor_tensor(tt, four(7), mask(K_N2), ALU.mult)
                    v.tensor_tensor(ttT, lbT, mask(K_N2T), ALU.mult)
                    step(v.tensor_tensor(loT, lbT, mask(K_OFF), ALU.mult))
                    v.tensor_tensor(tt, tt, mask(K_ID), ALU.add)
                    v.tensor_tensor(ttT, ttT, mask(K_ID), ALU.add)
                    v.tensor_tensor(mrkT, span(3)[:, :, 128:256], mask(K_MI), ALU.mult)
                    evac(v.tensor_tensor(mrbT, span(5)[:, :, 128:256], mask(K_MI), ALU.mult), f"S{name}")
                    v.tensor_copy(rhs[:, :, 0:64], toks[:, 0, :].rearrange("p (m e c) -> p m e c", m=4, e=2)[:, :, par_, :])
                    v.wait_ge(rk_mm, mm_at(l, f"LV{name}"))
                    v.tensor_copy(rhs[:, :, 64:128], ps[:, 6, 0:256].rearrange("p (m c) -> p m c", m=4)).then_inc(t_ok, 1)
                    for i in range(LV):
                        last = i == LV - 1
                        v.wait_ge(rk_mm, mm_at(l, f"X{name}{i}"))
                        if not last:
                            step(v.tensor_tensor(loT, lbT, mask(K_OFF + (i + 1) * P), ALU.mult))
                        lo(l, u0 + i + 3)
                        if not last:
                            v.wait_ge(rk_mm, mm_at(l, f"T{name}{i}"))
                            v.tensor_tensor(tt, tt, four(5), ALU.subtract).then_inc(t_ok, 1)
                            v.wait_ge(t_ok, l * N_T + g * LV + i + 2)
                        v.wait_ge(rk_mm, mm_at(l, f"TT{name}{i}"))
                        v.tensor_tensor(ttT, ttT, four(4), ALU.subtract).then_inc(rk_ev, 1)
                        if i in (1, 4):
                            merge_gb(u0 + i + 1)
                    v.wait_ge(rk_mm, mm_at(l, f"ZG{name}"))
                    p0 = 64 * par_
                    rows = slice(p0, p0 + 64)
                    z = four(3)
                    t0 = CHUNK if b == 0 else 0
                    v.tensor_tensor(zT[rows, :, b * P + t0 - CHUNK:(b + 1) * P - CHUNK], ar[rows, :, b, 1, t0:P], z[0:64, :, t0:P], ALU.subtract)
                    ins = v.tensor_scalar(y[rows, 0:4, b * P:(b + 1) * P], z[64:128], -1.0, None, ALU.mult)
                    for c in range(2):
                        q = 2 * b + c
                        o = ps[rows, 4 + c, :].rearrange("p (e m c) -> p e m c", e=2, m=4)
                        if q < NCH - 1:
                            ins = v.tensor_tensor(hP[rows, q, :, :], o[:, 0, :, :], pc[rows, :, q:q + 1].broadcast_to([64, 4, 64]), ALU.mult)
                        if 0 < q < NCH - 1:
                            ins = v.tensor_tensor(gT[rows, q - 1, :, :], cn[rows, K_ID + p0:K_ID + p0 + 64]
                                                  .rearrange("p (a t) -> p a t", a=1).broadcast_to([64, 4, 64]), o[:, 1, :, :], ALU.subtract)
                    evac(ins, f"ZG{name}")
                evac(v.tensor_scalar(st[:, 0, :, :], hP[:, 0, :, :], -1.0, None, ALU.mult), "st0")
                lo(l, U_GR + 2)
                for q in range(1, NCH - 1):
                    v.wait_ge(rk_mm, mm_at(l, f"st{q}"))
                    for p0 in (0, 64):
                        ins = v.tensor_tensor(stn[p0:p0 + 64], ps[p0:p0 + 64, 3 + p0 // 64, 0:256].rearrange("p (m c) -> p m c", m=4),
                                              pc[p0:p0 + 64, :, q:q + 1].broadcast_to([64, 4, 64]), ALU.mult)
                    step(ins)
                    evac(v.tensor_tensor(st[:, q, :, :], stn, hP[:, q, :, :], ALU.subtract), f"st{q}")
                    lo(l, U_GR + 2 + q)
                v.memset(proj[:, T_R:T_R + 3, 0:1], 0.0)
                ya = y[:, 0:4, :]
                v.wait_ge(rk_mm, mm_at(l, "y"))
                for p0 in (0, 64):
                    ins = v.tensor_tensor(ya[p0:p0 + 64, :, CHUNK:], ya[p0:p0 + 64, :, CHUNK:],
                                          span(3 + p0 // 32)[p0:p0 + 64, :, CHUNK:], ALU.add)
                evac(ins, "y")
                lo(l, U_GR + 5)
                v.wait_ge(rk_mm, mm_at(l, "mean"))
                step(v.scalar_tensor_tensor(ya, span(3), -1.0 / HD, ya, ALU.mult, ALU.add))
                evac(v.tensor_tensor(tmp, ya, ya, ALU.mult), "mean")
                lo(l, U_GR + 6)
                v.wait_ge(rk_mm, mm_at(l, "var"))
                step(v.tensor_scalar(tmp, span(5), 1.0 / HD, 64e-5, ALU.mult, ALU.add))
                evac(v.reciprocal(tmp, tmp), "var")
                lo(l, U_GR + 7)
                piece(l * 3 + 2, 0)
                v.wait_ge(exp_ok, l * 3 + 3)
                step(v.tensor_tensor(ya, ya, tmp, ALU.mult))
                for m in range(4):
                    ins = v.tensor_scalar(y[:, m, :], y[:, m, :], pr[:, C_GW + m:C_GW + m + 1],
                                          pr[:, C_GB + m:C_GB + m + 1], ALU.mult, ALU.add)
                step(ins)
                lo(l, U_GR + 8)
                step(v.tensor_tensor(ya, ya, bon, ALU.add))
                v.tensor_tensor(ya, ya, gg, ALU.mult).then_inc(in_ok, 1)
                lo(l, U_GR + 9)
                sub_split(l * (N_SPLIT + 1) + 6, sl[:, :, :], ya, sh[:, :, :])
                for i in range(4):
                    lo(l, U_BR + i + 2)
                    tiles = slice(2 * i, 2 * i + 2)
                    v.wait_ge(a_free, a_at(l, U_GR + 7))
                    v.wait_ge(unit_done, done(l, U_BR + i))
                    step(v.tensor_tensor(gr[:, tiles, :], two((U_BR + i) % RING), gr[:, tiles, :], ALU.mult))
                    v.tensor_tensor(merged[:, tiles, :], merged[:, tiles, :], gr[:, tiles, :], ALU.add).then_inc(v_free, 1)
                    v.wait_ge(v_free, v_at(l, U_BR + i))
                    v.sem_inc(mg_ok, 1)
                    v.wait_ge(hh_ok, l * N_H + H_MG + i + 1)
                    v.tensor_tensor(hl[:, tiles, :], merged[:, tiles, :], hh[:, tiles, :], ALU.subtract).then_inc(h_ok, 1)
                for k in range(KT):
                    lo(l, U_WO + k + 2)
                    if k < KT - 1:
                        piece(l * 3 + 2, k + 1)
                    v.wait_ge(unit_done, done(l, U_WO + k))
                    v.scalar_tensor_tensor(x[:, k, :], ps[:, (U_WO + k) % RING, 0:SEQ], mod[:, 16 + k:17 + k], x[:, k, :],
                                           ALU.mult, ALU.add).then_inc(v_free, 1)
                mod_third(l * 3 + 2, 7, mod[:, 32:48], pr[:, C_BADA + 32:C_BADA + 48])
                v.wait_ge(v_free, v_at(l, U_WO + KT - 1))
                norm(3, C_N2, 32, 24, H_N2)

                outer = base[0]

                def taps(j, r):
                    v.wait_ge(cv_ok, l * FT + j + 1)
                    for e in range(2):
                        src, dst = two(r)[:, e, :], cg[:, r, e, :]
                        step(v.scalar_tensor_tensor(dst[:, 1:], src[:, 0:SEQ - 1], pr[:, bass.ds(C_CW + (2 + e) * FT + j, 1)],
                                                    dst[:, 1:], ALU.mult, ALU.add))
                        v.scalar_tensor_tensor(dst[:, 2:], src[:, 0:SEQ - 2], pr[:, bass.ds(C_CW + e * FT + j, 1)],
                                               dst[:, 2:], ALU.mult, ALU.add).then_inc((cv2_ok, taps_ok)[e], 1)

                def multiply(j, r):
                    v.wait_ge(taps_ok, l * FT + j + 1 + 4)
                    v.wait_ge(si_ok, l * FT + j + 1)
                    v.tensor_tensor(sg[:, r, :], sg[:, r, :], cg[:, r, 1, :], ALU.mult).then_inc(mul_ok, 1)

                def act_lo(j, r):
                    v.wait_ge(ah_ok, l * FT + j + 1)
                    v.tensor_tensor(sl[:, r, :], sg[:, r, :], sh[:, r, :], ALU.subtract).then_inc(act_ok, 1)

                for j in range(2):
                    lo(l, U_FF + 2 * j + 2)
                    lo(l, U_FF + 2 * j + 3)
                    if j:
                        act_lo(0, 0)
                    taps(j, j)
                    multiply(j, j)
                piece(l * 3 + 3, 0)
                per = 8
                with v.Fori(0, (FT - 2) // 4) as i:
                    base[0] = outer + i * per
                    start = count[0]
                    for o in range(4):
                        j, r = 2 + 4 * i + o, (2 + o) % 4

                        def lo_ff(e):
                            s = (U_FF + 3 * o + e) % RING
                            v.wait_ge(hi_ok, l * N_UNITS + i * 12 + U_FF + 6 + 3 * o + e + 1)
                            v.tensor_tensor(wl[:, s, :], raw[:, s, :], wh[:, s, :], ALU.subtract).then_inc(lo_ok, 1)

                        lo_ff(0)
                        lo_ff(1)
                        act_lo(j - 1, (r + 3) % 4)
                        taps(j, r)
                        lo_ff(2)
                        multiply(j, r)
                        if o == 2:
                            piece(l * 3 + 3, i + 1, first=False)
                    assert count[0] - start == per
                base[0] = outer
                count[0] += 4 * per
                act_lo(FT - 1, (FT - 1) % 4)
                piece(l * 3 + 3, 6)
                piece(l * 3 + 3, 7)
                lo(l, N_UNITS)
                lo(l, N_UNITS + 1)
                mod_third(l * 3 + 3, 3, mod[:, 0:16], parall[:, 1, C_BADA:C_BADA + 16])
                for k in range(KT):
                    if k == KT - 2:
                        v.wait_ge(unit_done, done(l, N_UNITS - 1))
                    elif k % 2 == 0:
                        v.wait_ge(dn_ps, l * 3 + k // 2 + 1)
                    v.scalar_tensor_tensor(x[:, k, :], two(4 + k // 2)[:, k % 2, :], mod[:, 40 + k:41 + k], x[:, k, :],
                                           ALU.mult, ALU.add).then_inc(x_ok, 1)
                v.wait_ge(x_ok, l * KT + KT)
            assert count[0] == N_DV, count[0]

            base[0], count[0] = DEPTH * N_DV + pre, 0
            v.tensor_tensor(sq, x[:, :, :], x[:, :, :], ALU.mult).then_inc(sq_ok, 1)
            inv_square(DEPTH * N_NORM + 1, 3, 1, D_MODEL)
            for k in range(KT):
                ins = v.scalar_tensor_tensor(sq[:, k, :], x[:, k, :], cn[:, K_FG + k:K_FG + k + 1], rs[:, 0, :], ALU.mult, ALU.mult)
            ins.then_inc(fin_ok, 1)

        @block.tensor
        def _(pe):
            def mm(o, lhsT, rhs_, start=True, stop=True):
                return pe.matmul(o, lhsT, rhs_, start=start, stop=stop)

            def mm3(o, lhs, rh, start, stop, skip=False):
                (lh, ll), (rh_, rl) = lhs, rh
                pe.matmul(o, lh, rh_, start=start, stop=False, skip_group_check=skip)
                pe.matmul(o, lh, rl, start=False, stop=False, skip_group_check=skip)
                return pe.matmul(o, ll, rh_, start=False, stop=stop, skip_group_check=skip)

            def weights(s, c, n=P, rows=slice(0, P)):
                return wh[rows, s, c:c + n], wl[rows, s, c:c + n]

            def wide(k, cols=slice(0, SEQ)):
                return hh[:, k, cols], hl[:, k, cols]

            def narrow(k, cols=slice(0, SEQ), rows=slice(0, P)):
                return sh[rows, k, cols], sl[rows, k, cols]

            def arrived(l, u):
                pe.wait_ge(lo_ok, l * N_UNITS + u + 1 + RING)

            def bank_free(l, u):
                if u in V_PLACE:
                    pe.wait_ge(v_free, v_at(l, u))
                else:
                    pe.wait_ge(a_free, a_at(l, u))

            def tile(s, half=None):
                for k in range(KT) if half is None else range(half * 4, half * 4 + 4):
                    last = mm3(ps[:, s, 0:SEQ], weights(s, k * P), wide(k), k == 0, k == KT - 1)
                return last

            def branch(s, j):
                for k in range(4):
                    last = mm3(two(s)[:, j, :], weights(s, (j * 4 + k) * P), narrow(k), k == 0, k == 3)
                return last

            def mod_sum(t, bank):
                pe.wait_ge(ada_used, (t + 1) * KT + 2)
                for m in range(16):
                    last = mm(ps[:, bank, m:m + 1], acc[:, m * P:(m + 1) * P], ones[:, 0:1])
                last.then_inc(mod_ps, 1)

            def sumsq(nth):
                pe.wait_ge(sq_ok, nth)
                for k in range(KT):
                    last = mm(ps[:, 3, 0:SEQ], ones, sq[:, k, :], k == 0, k == KT - 1)
                last.then_inc(ss_ps, 1)

            mod_sum(0, 3)
            with pe.Fori(0, DEPTH) as l:
                def rk(name):
                    return ev_at(l, name)

                pe.wait_ge(mod_ok, l * 3 + 1)
                sumsq(l * N_NORM + 1)
                pe.wait_ge(h_ok, l * N_H + KT)
                alone(pe)
                with pe.Fori(0, 5) as i:
                    for s in range(RING):
                        pe.wait_ge(lo_ok, l * N_UNITS + i * RING + s + 1 + RING)
                        pe.wait_ge(a_free, l * N_A + i * RING + s + 1)
                        tile(s).then_inc(unit_done, 1)

                def full(u):
                    arrived(l, u)
                    bank_free(l, u - RING)
                    tile(u % RING).then_inc(unit_done, 1)

                for u in range(15, 19):
                    full(u)
                arrived(l, U_LORA)
                bank_free(l, U_LORA - RING)
                pe.wait_ge(sl_ok, l * N_SPLIT + S_LORA)
                s = U_LORA % RING
                for m in range(4):
                    mm3(span(3)[:, m, :], weights(s, m * P, rows=slice(0, 64)), narrow(0, rows=slice(0, 64)), True, True)
                    mm3(span(5)[:, m, :], weights(s, m * P, rows=slice(64, 128)), narrow(0, rows=slice(64, 128)), True, True)
                for m in range(4):
                    last = mm3((two(7), two(s))[m // 2][:, m % 2, :], weights(s, 512 + m * P), narrow(1), True, True)
                last.then_inc(unit_done, 1)
                u = U_LORA + 1
                arrived(l, u)
                bank_free(l, u - RING)
                for m in range(4):
                    if m == 2:
                        pe.wait_ge(lora_ev, l * 10 + 2)
                    last = mm3((two(u % RING), two(3))[m // 2][:, m % 2, :], weights(u % RING, m * P, rows=slice(32, 64)),
                               narrow(2, rows=slice(32, 64)), True, True)
                last.then_inc(unit_done, 1)
                full(21)
                pe.wait_ge(kq_ok, l + 1)
                pe.wait_ge(lora_ev, l * 10 + 10)
                for e in range(2):
                    last = mm(ps[:, 5 + e, :], blk, sqk[:, 2 * e:2 * e + 2, :].rearrange("p a t -> p (a t)"))
                last.then_inc(rk_mm, 1)
                full(22)
                pe.wait_ge(sq_ok, l * N_NORM + 2)
                for k in range(4):
                    last = mm(two(7)[:, k // 2, :], ones, sq[:, k, :], k % 2 == 0, k % 2 == 1)
                last.then_inc(ss_ps, 1)
                full(23)
                full(24)
                pe.wait_ge(rk_ev, rk("ready"))
                for e in range(2):
                    last = mm(ps[:, 3 + e, :], blk, bon[:, 2 * e:2 * e + 2, :].rearrange("p a t -> p (a t)"))
                last.then_inc(rk_mm, 1)
                full(25)
                pe.wait_ge(rec_ok, l * N_NORM + 2)
                mod_sum(l * 3 + 1, 7)
                for u in range(26, U_FV):
                    full(u)
                for e in range(2):
                    u = U_FV + 2 * e
                    arrived(l, u + 1)
                    bank_free(l, U_FV - 2 - e)
                    for b in range(TB):
                        for k in range(KT):
                            last = mm3(two((u + 1) % RING)[:, b, :], wide(k, slice(b * P, (b + 1) * P)),
                                       weights((u + k // 4) % RING, k % 4 * 256, 256), k == 0, k == KT - 1)
                    last.then_inc(unit_done, 2)
                pe.wait_ge(sl_ok, l * N_SPLIT + S_LAT)
                pe.wait_ge(rk_ev, rk("bon"))
                for e in range(2):
                    u = U_QUP + e
                    arrived(l, u)
                    for hd in range(4):
                        for k in range(2):
                            last = mm3(span(5 - 2 * e)[:, hd, :], weights(u % RING, (k * 4 + hd) * P), narrow(k), k == 0, k == 1)
                    last.then_inc(unit_done, 1)
                arrived(l, U_KUP)
                pe.wait_ge(rope_ok, l * 2 + 1)
                for m in range(4):
                    for k in range(2):
                        last = mm3(span(5)[:, m, :], weights(U_KUP % RING, k * 512 + m * P), narrow(2 + k), k == 0, k == 1)
                last.then_inc(unit_done, 1)
                arrived(l, U_VUP)
                pe.wait_ge(rope_ok, l * 2 + 2)
                for b in range(TB):
                    for k in range(2):
                        last = mm3(ps[:, 3 + b, :], narrow(2 + k, slice(b * P, (b + 1) * P)), weights(U_VUP % RING, k * 512, 512), k == 0, k == 1)
                last.then_inc(unit_done, 1)
                pe.wait_ge(fl_dma, l * 32 + 32)
                pe.wait_ge(up_ok, l * 5 + 5)
                bank_free(l, U_FV + 3)
                alone(pe)

                def scores(n):
                    if n >= 2:
                        pe.wait_ge(s_ok, l * 2 * H + n - 1)
                    for b in range(TB):
                        o = ps[:, n % 2, 128 * b:128 + 256 * b]
                        nk = P * (b + 1)
                        if n < H:
                            p0 = 64 * (n % 2)
                            mm(o, proj[p0:p0 + 64, T_FQ + n // 2, 1 + b * P:1 + (b + 1) * P],
                               proj[p0:p0 + 64, T_FK + n // 2, 1:1 + nk], True, False)
                            last = mm(o, fa[:, n, b * P:(b + 1) * P], fb[:, n, 0:nk], False, True)
                        else:
                            last = mm(o, qh[:, n - H, b * P:(b + 1) * P], kh[:, n - H, 0:nk])
                    last.then_inc(s_ps, 1)

                def products(n):
                    pe.wait_ge(pn_ok, l * 2 * H + n + 1)
                    if n >= 2:
                        pe.wait_ge(pt_ok, l * 2 * H + n - 1)
                    for j in range(3):
                        last = pe.transpose(ps[:, 2 + n % 2, j * P:(j + 1) * P], pp[:, n % 2, j * P:(j + 1) * P], ident)
                    last.then_inc(pt_ps, 1)
                    pe.wait_ge(pt_ok, l * 2 * H + n + 1)
                    if n >= 4:
                        pe.wait_ge(o_ok, l * H + n // 2 - 1)
                    vv = vf if n < H else vm
                    hd = n % H
                    o = ps[64 * (n % 2):64 * (n % 2) + 64, 4 + n // 2 % 2, 0:SEQ]
                    mm(o[:, 0:P], vv[:, 0, hd * 64:(hd + 1) * 64], pT[:, n % 2, 0:P])
                    mm(o[:, P:SEQ], vv[:, 0, hd * 64:(hd + 1) * 64], pT[:, n % 2, P:2 * P], True, False)
                    mm(o[:, P:SEQ], vv[:, 1, hd * 64:(hd + 1) * 64], pT[:, n % 2, 2 * P:3 * P], False, True).then_inc(o_ps, 1)

                scores(0)
                for n in range(2 * H):
                    if n + 1 < 2 * H:
                        scores(n + 1)
                    products(n)
                pe.wait_ge(s_ok, l * 2 * H + 2 * H)
                pe.wait_ge(o_ok, l * H + H)
                pe.wait_ge(rk_ev, rk("rho"))
                alone(pe)

                for g, (b, par_) in enumerate(GROUPS):
                    name = f"{b}{par_}"
                    rows = slice(64 * par_, 64 * par_ + 64)
                    t0 = b * P

                    def half(n):
                        u, e = U_GB + 6 * g + n // 2, n % 2
                        pair = (u - U_GB) % 3 == 2
                        if e == 0:
                            arrived(l, u)
                            if u >= U_GB + RING:
                                bank_free(l, u - RING)
                            if pair:
                                pe.wait_ge(sl_ok, l * N_SPLIT + (S_FOX if g < 2 else S_MLA))
                        last = branch(u % RING, e) if pair else tile(u % RING, e)
                        if e:
                            last.then_inc(unit_done, 1)

                    if par_ == 0:
                        if b:
                            pe.wait_ge(rk_ev, rk(f"tr{b}") - 1)
                            alone(pe)
                        for m in range(4):
                            for i, srcv in enumerate((ar[:, m, b, 0, :], bet[:, m, t0:t0 + P], kap[:, m, t0:t0 + P],
                                                      proj[:, T_V + m, 1 + t0:1 + t0 + P])):
                                last = pe.transpose(ps[:, 3 + i, m * P:(m + 1) * P], srcv, ident)
                        last.then_inc(rk_mm, 1)
                        half(0)
                    pe.wait_ge(rk_ev, rk(f"S{name}") - 1)
                    alone(pe)
                    for m in range(4):
                        arb = ar[rows, m, b, :, :].rearrange("p e t -> p (e t)")
                        mm(span(3)[:, m, :], kap[rows, m, t0:t0 + P], arb)
                        mm(span(5)[:, m, :], bet[rows, m, t0:t0 + P], arb)
                        last = mm(four(7)[:, m, :], ar[rows, m, b, 0, :], bet[rows, m, t0:t0 + P])
                    last.then_inc(rk_mm, 1)
                    if par_:
                        half(0)
                    half(1)
                    pe.wait_ge(rk_ev, rk(f"S{name}"))
                    for m in range(4):
                        hd = 2 * m + par_
                        last = mm(ps[:, 6, m * 64:(m + 1) * 64], lakT[:, m, :], toks[:, 3, hd * 64:(hd + 1) * 64])
                    last.then_inc(rk_mm, 1)
                    for i in range(LV):
                        if i:
                            pe.wait_ge(t_ok, l * N_T + g * LV + i + 1)
                        for m in range(4):
                            last = mm(four(3)[:, m, :], loT[:, m, :], tt[:, m, :])
                        last.then_inc(rk_mm, 1)
                        half(2 + 2 * i)
                        pe.wait_ge(rk_ev, rk(f"X{name}{i}"))
                        if i < LV - 1:
                            for m in range(4):
                                last = mm(four(5)[:, m, :], ttT[:, m, :], xx[:, m, :])
                            last.then_inc(rk_mm, 1)
                        for m in range(4):
                            last = mm(four(4)[:, m, :], xx[:, m, :], ttT[:, m, :])
                        last.then_inc(rk_mm, 1)
                        half(3 + 2 * i)
                    pe.wait_ge(rk_ev, rk(f"TT{name}{LV - 1}"))
                    pe.wait_ge(t_ok, l * N_T + (g + 1) * LV)
                    for m in range(4):
                        last = mm(four(7)[:, m, :], ttT[:, m, :], rhs[:, m, :])
                    last.then_inc(rk_mm, 1)
                    pe.wait_ge(rk_ev, rk(f"WU{name}"))
                    alone(pe)
                    for m in range(4):
                        hd = 2 * m + par_
                        mm(four(3)[:, m, :], wu[:, m, :], mrbT[:, m, :], True, False)
                        last = mm(four(3)[:, m, :], v0n[:, hd, :], mrkT[:, m, :], False, True)
                        for c in range(2):
                            q = 2 * b + c
                            r = slice(64 * c, 64 * c + 64)
                            bt = toks[r, 1, hd * 64:(hd + 1) * 64]
                            kt = toks[r, 2, hd * 64:(hd + 1) * 64]
                            if q < NCH - 1:
                                o = ps[rows, 4 + c, m * 64:(m + 1) * 64]
                                mm(o, bt, wu[r, m, 64:128], True, False)
                                last = mm(o, kt, v0n[r, hd, 64:128], False, True)
                            if 0 < q < NCH - 1:
                                last = mm(ps[rows, 4 + c, 256 + m * 64:256 + (m + 1) * 64], wu[r, m, 0:64], bt)
                    last.then_inc(rk_mm, 1)
                gates_r = iter(range(U_GR, U_BR))
                full(next(gates_r))
                for q in range(1, NCH - 1):
                    pe.wait_ge(rk_ev, rk(f"st{q - 1}"))
                    alone(pe)
                    for m in range(4):
                        for p0 in (0, 64):
                            last = mm(ps[p0:p0 + 64, 3 + p0 // 64, m * 64:(m + 1) * 64], gT[p0:p0 + 64, q - 1, m, :], st[p0:p0 + 64, q - 1, m, :])
                    last.then_inc(rk_mm, 1)
                    full(next(gates_r))
                pe.wait_ge(rk_ev, rk("st2"))
                alone(pe)
                for m in range(4):
                    for q in range(1, NCH):
                        for p0 in (0, 64):
                            last = mm(span(3 + p0 // 32)[p0:p0 + 64, m, q * CHUNK:(q + 1) * CHUNK], st[p0:p0 + 64, q - 1, m, :],
                                      zT[p0:p0 + 64, m, (q - 1) * CHUNK:q * CHUNK])
                last.then_inc(rk_mm, 1)
                full(next(gates_r))
                pe.wait_ge(rk_ev, rk("y"))
                for e in range(2):
                    last = mm(ps[:, 3 + e, :], blk, y[:, 2 * e:2 * e + 2, :].rearrange("p a t -> p (a t)"))
                last.then_inc(rk_mm, 1)
                full(next(gates_r))
                pe.wait_ge(rk_ev, rk("mean"))
                for e in range(2):
                    last = mm(ps[:, 5 + e, :], blk, tmp[:, 2 * e:2 * e + 2, :].rearrange("p a t -> p (a t)"))
                last.then_inc(rk_mm, 1)
                for u in gates_r:
                    full(u)
                pe.wait_ge(sl_ok, l * N_SPLIT + S_RW)
                for i in range(4):
                    u = U_BR + i
                    arrived(l, u)
                    bank_free(l, u - RING)
                    for j in range(2):
                        last = branch(u % RING, j)
                    last.then_inc(unit_done, 1)
                pe.wait_ge(h_ok, l * N_H + H_MG + 4)
                for u in range(U_WO, U_FF):
                    full(u)
                mod_sum(l * 3 + 2, 7)
                zero = cn[:, K_CAUS:K_CAUS + P]
                for b in range(3):
                    pe.matmul(ps[:, 4 + b, :], zero, cn[:, 0:512], start=True, stop=False, skip_group_check=True)
                sumsq(l * N_NORM + 3)
                pe.wait_ge(mod_ok, l * 3 + 3)
                pe.matmul(ps[:, 7, :], zero, cn[:, 0:512], start=True, stop=False, skip_group_check=True)
                pe.wait_ge(h_ok, l * N_H + N_H)

                def up(s, e, n, j, r):
                    pe.wait_ge(lo_ok, n + 1 + RING)
                    if e == 0:
                        pe.wait_ge(taps_ok, l * FT + j + 1)
                    for k in range(KT):
                        last = mm3(two(r)[:, e, :], weights(s, k * P), wide(k), k == 0, k == KT - 1)
                    last.then_inc(unit_done, 1)

                def down(s, n, j, r, final=False):
                    pe.wait_ge(lo_ok, n + 1 + RING)
                    pe.wait_ge(act_ok, l * FT + j + 1)
                    for m in range(KT):
                        last = mm3(two(4 + m // 2)[:, m % 2, :], weights(s, m * P), narrow(r), False, final, skip=True)
                        if final and m in (1, 3, 5):
                            last.then_inc(dn_ps, 1)
                    last.then_inc(unit_done, 1)

                for j in range(2):
                    for e in range(2):
                        up((U_FF + 2 * j + e) % RING, e, l * N_UNITS + U_FF + 2 * j + e, j, j)
                with pe.Fori(0, (FT - 2) // 4) as i:
                    for o in range(4):
                        j, r = 2 + 4 * i + o, (2 + o) % 4
                        n = l * N_UNITS + i * 12 + U_FF + 4 + 3 * o
                        for e in range(2):
                            up((U_FF + 4 + 3 * o + e) % RING, e, n + e, j, r)
                        down((U_FF + 6 + 3 * o) % RING, n + 2, j - 2, o)
                u = down_unit(FT - 2)
                down(u % RING, l * N_UNITS + u, FT - 2, (FT - 2) % 4)
                mod_sum(l * 3 + 3, 3)
                u += 1
                down(u % RING, l * N_UNITS + u, FT - 1, (FT - 1) % 4, final=True)
            pe.wait_ge(mod_ok, DEPTH * 3 + 1)
            sumsq(DEPTH * N_NORM + 1)


N_DV = 145


def _constants():
    c = np.zeros((P, N_CON), np.float32)
    i = np.arange(P)
    s, t = i[:, None], i[None, :]
    same = s // CHUNK == t // CHUNK
    c[:, K_ID:K_ID + P] = np.eye(P)
    c[:, K_ONES:K_ONES + SEQ] = 1
    c[:, K_BLK:K_BLK + P] = s // 64 == t // 64
    c[:, K_MS:K_MS + P] = same & (s < t)
    c[:, K_MI:K_MI + P] = same & (s <= t)
    c[:, K_N2T:K_N2T + P] = -1.0 * ((s // 2 == t // 2) & (s < t))
    c[:, K_N2:K_N2 + P] = -1.0 * ((s // 2 == t // 2) & (s > t))
    for n, w in enumerate(LEVELS):
        c[:, K_OFF + n * P:K_OFF + (n + 1) * P] = (s // (2 * w) == t // (2 * w)) & (s // w < t // w)
    c[:, K_CAUS + P:K_CAUS + 2 * P] = np.where(s >= t, 0, NEG)
    c[:, K_RST:K_RST + SEQ] = np.arange(SEQ)[None, :] % CHUNK != 0
    inv = np.power(np.float32(10000.0), -np.arange(16, dtype=np.float32) / np.float32(16))
    c[:, K_TRIG] = inv[i % 16]
    cos = i < 96
    c[:, K_TRIG + 1] = np.where(cos, 0.25, 0.0)
    c[:, K_TRIG + 2] = np.where(cos, np.pi / 2, 0.0)
    c[:, K_TRIG + 3] = np.where(cos | (i % 32 >= 16), 1.0, -1.0)
    return c


def _tiles(w):
    k, n = w.shape
    return w.reshape(k // P, P, n // P, P).transpose(1, 2, 0, 3)


def kernel(**inputs):
    import concourse.bacc as bacc
    from concourse.bass_utils import run_bass_kernel_spmd as run

    f = {k: np.asarray(v) for k, v in inputs.items()}
    cols = lambda v: v.reshape(-1, P).T
    units = np.zeros((DEPTH * N_UNITS + AHEAD, P, UNIT), np.float32)
    par = np.zeros((P, DEPTH, N_PAR), np.float32)
    for l in range(DEPTH):
        w = f["w_in"][l]
        put = lambda u, a: units[l * N_UNITS + u].__setitem__((slice(None), slice(0, a.reshape(P, -1).shape[1])), a.reshape(P, -1))
        r0, wl, k0, v0, al, gl = 0, 512, 576, 1088, 1600, 1664
        fq, fk, fv, ff, mq, mkv, mkr, gt = 1792, 2304, 2816, 3328, 3336, 3592, 3848, 3880
        mix = np.zeros((D_MODEL, P), np.float32)
        mix[:, 0:8] = w[:, ff:ff + 8]
        if l:
            mix[:, 32:64] = f["rw_vres_down"][l - 1]
        mix[:, 64:96] = w[:, mkr:mkr + 32]
        mix[:, 96:112], mix[:, 112:128] = w[:, mkr + 16:mkr + 32], w[:, mkr:mkr + 16]
        feat = np.concatenate([mix, w[:, wl:wl + 64], w[:, al:al + 64], w[:, gl:gl + 128], w[:, r0:r0 + 512],
                               w[:, k0:k0 + 512], w[:, v0:v0 + 512], w[:, mq:mq + 512], w[:, fq:fq + 1024]], 1)
        ft = _tiles(feat)
        for u in range(N_FEAT):
            put(u if u < U_LORA else u + 2, ft[:, u])
        for u in range(4):
            c, k = u // 2 * 256, u % 2 * 512
            put(U_FV + u, w[k:k + 512, fv + c:fv + c + 256].reshape(4, P, 256).transpose(1, 0, 2))
        lo = np.zeros((P, 2 * UNIT), np.float32)
        lo[0:64, 0:512], lo[64:128, 0:512] = f["rw_w_up"][l], f["rw_a_up"][l]
        lo[:, 512:1024] = f["rw_g_up"][l]
        if l:
            lo[32:64, 1024:1536] = f["rw_vres_up"][l - 1]
        put(U_LORA, lo[:, :UNIT])
        put(U_LORA + 1, lo[:, UNIT:])
        q = f["mla_w_q_up"][l].reshape(2, P, H, 96).transpose(1, 0, 2, 3)
        q = np.concatenate([q, q[..., 80:96], q[..., 64:80]], 3)
        put(U_QUP, q[:, :, 0:4])
        put(U_QUP + 1, q[:, :, 4:8])
        kv = f["mla_w_kv_up"][l].reshape(2, P, H, 2, 64).transpose(1, 0, 3, 2, 4)
        put(U_KUP, kv[:, :, 0])
        put(U_VUP, kv[:, :, 1])
        gw = _tiles(w[:, gt:gt + 3072])
        bt = [_tiles(f["w_branch"][l, g]) for g in range(3)]
        for g in (1, 2):
            for i in range(4):
                u = U_GB + ((g - 1) * 4 + i) * 3
                put(u, gw[:, g * 8 + 2 * i])
                put(u + 1, gw[:, g * 8 + 2 * i + 1])
                put(u + 2, bt[g][:, 2 * i:2 * i + 2])
        for t in range(KT):
            put(U_GR + t, gw[:, t])
        for i in range(4):
            put(U_BR + i, bt[0][:, 2 * i:2 * i + 2])
        wo = _tiles(f["w_o"][l])
        for t in range(KT):
            put(U_WO + t, wo[:, t])
        up = _tiles(f["ffn_w_up"][l])
        dn = f["ffn_w_down"][l].reshape(FT, P, D_MODEL).transpose(1, 0, 2)
        for t in range(FT):
            put(up_unit(t), up[:, t])
            put(up_unit(t) + 1, up[:, FT + t])
            put(down_unit(t), dn[:, t])
        p = par[:, l]
        p[:, C_N1:C_N1 + 8], p[:, C_N2:C_N2 + 8] = cols(f["norm1_g"][l]), cols(f["norm2_g"][l])
        p[:, C_BADA:C_BADA + 48] = cols(f["b_ada"][l])
        mu = f["mu_shift"][l]
        p[:, C_MU + 1:C_MU + 15] = cols(np.concatenate([mu[wl:wl + 64], mu[al:al + 64], mu[gl:gl + 128], mu[r0:r0 + 512],
                                                        mu[k0:k0 + 512], mu[v0:v0 + 512]]))
        for c, name in ((C_W0, "rw_w0"), (C_A0, "rw_a0"), (C_KK, "rw_k_k"), (C_KA, "rw_k_a"), (C_RK, "rw_r_k"),
                        (C_GW, "rw_gn_w"), (C_GB, "rw_gn_b")):
            p[:, c:c + 4] = cols(f[name][l])
        p[0:8, C_MIX] = f["fox_b_f"][l]
        if l:
            p[:, C_V0:C_V0 + 4] = cols(f["rw_v0"][l - 1])
            p[32:64, C_MU] = f["rw_vres_mu"][l - 1]
        p[:, C_MQ:C_MQ + 2], p[:, C_MKV:C_MKV + 2] = cols(f["mla_q_norm_g"][l]), cols(f["mla_kv_norm_g"][l])
        p[:, C_FLAG], p[:, C_FLAG + 1] = float(l > 0), float(l == 0)
        p[:, C_CW:C_CW + 132] = f["ffn_conv_w"][l].reshape(3 * 2 * FT, P).T
        p[:, C_CB:C_CB + 44] = cols(f["ffn_conv_b"][l])
    con = _constants()
    con[:, K_FG:K_FG + 8] = cols(f["final_g"])
    wa = f["w_ada"].reshape(DEPTH, KT, P, 3, 2048).transpose(0, 3, 1, 2, 4).reshape(DEPTH * 3 * KT, P, 2048)
    wa = np.concatenate([wa, wa[:KT]], 0)
    arrays = {
        "xT": f["x"][0].T.reshape(KT, P, SEQ).transpose(1, 0, 2),
        "cT": cols(f["c"][0]),
        "pos": np.broadcast_to(f["positions"], (P, SEQ)),
        "par": par, "con": con, "wada": wa, "ws": units,
    }
    arrays = {k: np.ascontiguousarray(a) for k, a in arrays.items()}
    nc = bacc.Bacc("TRN2", target_bir_lowering=False, num_devices=1)
    args = [nc.dram_tensor(k, a.shape, mybir.dt.from_np(a.dtype), kind="ExternalInput").ap() for k, a in arrays.items()]
    args.append(nc.dram_tensor("out", (P, KT, SEQ), F32, kind="ExternalOutput").ap())
    bass_trunk(nc, *args)
    res = run(nc, [arrays], core_ids=[0]).results[0]["out"]
    return res.transpose(1, 0, 2).reshape(D_MODEL, SEQ).T.reshape(1, SEQ, D_MODEL)
```

```python
from contextlib import ExitStack

import numpy as np

import concourse.bass as bass
from concourse import mybir

F32 = mybir.dt.float32
I32 = mybir.dt.int32
ALU = mybir.AluOpType
ACT = mybir.ActivationFunctionType

P = 128
D_MODEL, SEQ, DEPTH = 1024, 256, 2
KT = D_MODEL // P
TB = SEQ // P
H, HD = 8, 64
NOPE, ROPE = 64, 32
D_FF = 2816
FT = D_FF // P
CHUNK = 64
NCH = SEQ // CHUNK
UNIT = 1024
RING = 3
AHEAD = 2

T_MIX, T_WA, T_GL, T_R, T_K, T_V, T_MQ, T_MKV, T_FQ, T_FK = 0, 1, 2, 3, 7, 11, 15, 17, 19, 23
N_FEAT = 27

U_LORA, U_FV, U_QUP, U_KUP, U_VUP = 19, 29, 33, 35, 36
U_GB = 37
U_GR, U_GL, U_BR, U_WO, U_FF = 58, 63, 69, 73, 81
N_UNITS = U_FF + 3 * FT
assert N_UNITS % RING == 0

C_N1, C_N2, C_BADA, C_MU, C_W0, C_A0, C_V0 = 0, 8, 16, 64, 79, 83, 87
C_KK, C_KA, C_RK, C_GW, C_GB, C_MIX, C_MQ, C_MKV, C_FLAG = 91, 95, 99, 103, 107, 111, 112, 114, 116
C_CW, C_CB = 120, 252
N_PAR = 296

LEVELS = [2, 4, 8, 16, 32]
K_ID, K_ONES, K_BLK = 0, 128, 384
K_MS, K_MI, K_N2T, K_N2, K_OFF = 512, 640, 768, 896, 1024
K_CAUS, K_RST, K_TRIG, K_FG = 1664, 1920, 2176, 2180
N_CON = 2188

NEG = -1e30
RSQ_E = 0.6065306597126334
TWO_PI = 6.283185307179586
PI2_A, PI2_B = 6.28125, 0.0019350051879882812
PI2_C = TWO_PI - PI2_A - PI2_B
MAGIC = 12582912.0

def rk_order():
    mm, ev = ["ksq", "bonus"], ["ready", "bon", "rho"]
    for b in range(TB):
        mm.append(f"tr{b}")
        ev.append(f"tr{b}")
        for par in range(2):
            g = f"{b}{par}"
            mm += [f"N{g}", f"S{g}"]
            ev.append(f"S{g}")
            for i in range(len(LEVELS)):
                mm += [f"X{g}{i}"] + [f"T{g}{i}"] * (i < len(LEVELS) - 1) + [f"TT{g}{i}"]
                ev += [f"X{g}{i}", f"TT{g}{i}"]
            mm += [f"WU{g}", f"ZG{g}"]
            ev += [f"WU{g}", f"ZG{g}"]
    mm += [f"st{q}" for q in range(1, NCH - 1)] + ["y", "mean", "var"]
    ev += [f"st{q}" for q in range(NCH - 1)] + ["y", "mean", "var"]
    return [{n: i + 1 for i, n in enumerate(names)} for names in (mm, ev)]


RK_MM, RK_EV = rk_order()
N_MM, N_EV = len(RK_MM), len(RK_EV)


def gr_tile(u):
    return u - U_GR if u < U_GL else u - U_GR - 3


def up_unit(j):
    return U_FF + 2 * j if j < 2 else U_FF + 4 + 3 * (j - 2)


def down_unit(j):
    return U_FF + 6 + 3 * j if j < FT - 2 else N_UNITS - FT + j


V_UNITS = list(range(U_GB + 2, U_GR, 3)) + [U_GL + 2] + list(range(U_BR, U_FF))
A_UNITS = (list(range(U_FV)) + [U_FV + 1, U_FV + 3] + [u for u in range(U_GB, U_BR) if u not in V_UNITS])
A_PLACE = {u: i + 1 for i, u in enumerate(A_UNITS)}
V_PLACE = {u: i + 1 for i, u in enumerate(V_UNITS)}
N_A, N_V = len(A_UNITS), len(V_UNITS)

FV_BANKS = ((0, 5), (2, 6))

PIECES = (1, 1, 2, 1, 2, 1, 2, 1, 2, 1, 1, 1)

N_SPLIT = 5
S_LORA, S_LAT, S_FOX, S_MLA, S_RW = 1, 2, 3, 4, 5
N_H = 20
H_N1, H_MG, H_N2 = 0, 8, 12
N_NORM = 3
N_T = len(LEVELS) * 2 * TB
F32R = mybir.dt.float32r


def bass_trunk(nc, xT, cT, pos, par, con, wada, ws, out):
    ctx = ExitStack()
    with ctx:
        def sb(name, shape, dt=F32):
            return ctx.enter_context(nc.sbuf_tensor(name, shape, dt))

        def sem(name):
            return ctx.enter_context(nc.semaphore(name))

        raw = sb("raw", [P, RING, UNIT])
        wh = sb("wh", [P, RING, UNIT], F32R)
        wl = sb("wl", [P, RING, UNIT], F32R)
        x = sb("x", [P, KT, SEQ])
        hh = sb("hh", [P, KT, SEQ], F32R)
        hl = sb("hl", [P, KT, SEQ], F32R)
        sh = sb("sh", [P, 4, SEQ], F32R)
        sl = sb("sl", [P, 4, SEQ], F32R)
        proj = sb("proj", [P, N_FEAT, SEQ + 1])
        vf = sb("vf", [P, TB, 512])
        y = sb("y", [P, 12, SEQ])
        v1st = sb("v1st", [P, 4, SEQ])
        parall = sb("parall", [P, DEPTH, N_PAR])
        pr = sb("pr", [P, N_PAR])
        cn = sb("cn", [P, N_CON])
        mod = sb("mod", [P, 48])
        gain = sb("gain", [P, KT])
        ka1 = sb("ka1", [P, 4])
        cc = sb("cc", [P, KT])
        csig = sb("csig", [P, KT])
        rs = sb("rs", [P, 2, SEQ])
        posi = sb("posi", [P, SEQ], I32)
        trig = sb("trig", [P, SEQ])
        pc = sb("pc", [P, 4, NCH])
        mx, nb, den, rd = (sb(n, [P, 3, 2]) for n in ("mx", "nb", "den", "rd"))
        un = sb("un", [P, 9216])
        prep = sb("prep", [P, 9984])

        def view(t, at, *shape):
            n = int(np.prod(shape))
            v = t[:, at:at + n]
            if len(shape) == 1:
                return v
            if len(shape) == 2:
                return v.rearrange("p (a b) -> p a b", a=shape[0])
            return v.rearrange("p (a b c) -> p a b c", a=shape[0], b=shape[1])

        sq = view(un, 0, KT, SEQ)
        ada = (view(un, 2048, 2048), view(un, 6144, 2048))
        acc = view(un, 4096, 2048)
        acc2 = view(prep, 0, 2048)
        adb = (view(prep, 2048, 1024), y[:, 0:4, :].rearrange("p a t -> p (a t)"))
        shd = view(un, 6144, 3, SEQ)
        fac, sqk = view(un, 6144, 4, SEQ), view(un, 7168, 4, SEQ)
        vt = view(un, 8192, 4, SEQ)
        cum, tmp, kkn = (view(prep, i * 1024, 4, SEQ) for i in range(3))
        lgd, aa, kap, gg = (view(prep, 3072 + i * 1024, 4, SEQ) for i in range(4))
        tw = view(prep, 3072, 2, SEQ)
        bon, bet = lgd, aa
        ar = prep[:, 7168:9216].rearrange("p (m b e t) -> p m b e t", m=4, b=TB, e=2)
        zT = view(prep, 9216, 4, SEQ - CHUNK)
        tt, ttT, loT, xx, rhs, wu = (view(prep, i * 512, 4, P) for i in range(6))
        toks = view(un, 0, 4, 512)
        v0n = view(un, 2048, H, P)
        stn = view(un, 3072, 4, HD)
        st = view(un, 3328, NCH - 1, 4, HD)
        gT = view(un, 4096, NCH - 2, 4, HD)
        lakT, mrkT, lbT, mrbT = (view(un, 4608 + i * 512, 4, P) for i in range(4))
        hP = proj[:, T_R:T_R + 3, :].rearrange("p a t -> p (a t)")[:, 0:768].rearrange("p (q m c) -> p q m c", q=NCH - 1, m=4)
        qh = un[0:96, 0:2048].rearrange("p (h t) -> p h t", h=H)
        kh = un[0:96, 2048:4096].rearrange("p (h t) -> p h t", h=H)
        fa = un[96:98, 0:2048].rearrange("p (h t) -> p h t", h=H)
        fb = un[96:98, 2048:4096].rearrange("p (h t) -> p h t", h=H)
        vm = view(un, 4096, TB, 512)
        sc, pp, pT = (view(un, 5120 + i * 1152, 3 - i // 2, 384) for i in range(3))
        rtmp = un[64:96, 5120:7168].rearrange("p (h t) -> p h t", h=H)
        flog, ft, fcum, fneg = (un[0:8, 8192 + i * 256:8448 + i * 256] for i in range(4))
        lat = view(un, 1024, 4, SEQ)
        gate = view(un, 8704, 2, SEQ)
        gr = view(un, 0, KT, SEQ)
        merged = view(un, 6656, KT, SEQ)
        cg = un[:, 6144:8192].rearrange("p (j e t) -> p j e t", j=4, e=2)
        sg = view(un, 8192, 4, SEQ)

        ps = ctx.enter_context(nc.psum_tensor("ps", [P, 8, 512], F32))

        def done(l, u):
            return l * N_UNITS + u + 1 + RING

        def a_at(l, u):
            return l * N_A + A_PLACE[u] + RING

        def v_at(l, u):
            return l * N_V + V_PLACE[u]

        def mm_at(l, name):
            return l * N_MM + RK_MM[name]

        def ev_at(l, name):
            return l * N_EV + RK_EV[name]

        def two(bank):
            return ps[:, bank, :].rearrange("p (a t) -> p a t", a=2)

        def four(bank):
            return ps[:, bank, :].rearrange("p (a t) -> p a t", a=4)

        def span(bank):
            return ps[:, bank:bank + 2, :].rearrange("p b (a t) -> p (b a) t", a=2)

        landed = [sem(f"landed{s}") for s in range(RING)]
        hi_ok, lo_ok, unit_done = sem("hi_ok"), sem("lo_ok"), sem("unit_done")
        a_free, v_free = sem("a_free"), sem("v_free")
        loaded = sem("loaded")
        ada_first = [sem("ada_first0"), sem("ada_first1")]
        adb_in = [sem("adb_in0"), sem("adb_in1")]
        adb_used = sem("adb_used")
        sqx_ok = sem("sqx_ok")
        m_ok, tra_ok = sem("m_ok"), sem("tra_ok")
        ada_in, ada_used, mod_ps, mod_ok = sem("ada_in"), sem("ada_used"), sem("mod_ps"), sem("mod_ok")
        trig_r, trig_ok, csig_ok = sem("trig_r"), sem("trig_ok"), sem("csig_ok")
        dv, passed = sem("dv"), sem("passed")
        sq_ok, ss_ps, rec_ok, rt_ok = sem("sq_ok"), sem("ss_ps"), sem("rec_ok"), sem("rt_ok")
        t_norm, hh_ok, h_ok = sem("t_norm"), sem("hh_ok"), sem("h_ok")
        in_ok, sh_ok, sl_ok = sem("in_ok"), sem("sh_ok"), sem("sl_ok")
        shift_ok, lora_ev, kq_ok, fac_ok = sem("shift_ok"), sem("lora_ev"), sem("kq_ok"), sem("fac_ok")
        cum_ok, exp_ok = sem("cum_ok"), sem("exp_ok")
        rk_mm, rk_ev, t_ok = sem("rk_mm"), sem("rk_ev"), sem("t_ok")
        up_ok, rope_ok = sem("up_ok"), sem("rope_ok")
        fl_one = sem("fl_one")
        fl_in, fl_exp, fl_cum, fl_dma = sem("fl_in"), sem("fl_exp"), sem("fl_cum"), sem("fl_dma")
        s_ps, s_ok, p_ok, pn_ok = sem("s_ps"), sem("s_ok"), sem("p_ok"), sem("pn_ok")
        pt_ps, pt_ok, o_ps, o_ok = sem("pt_ps"), sem("pt_ok"), sem("o_ps"), sem("o_ok")
        mg_ok, x_ok = sem("mg_ok"), sem("x_ok")
        cv_ok, cv2_ok, taps_ok, si_ok = sem("cv_ok"), sem("cv2_ok"), sem("taps_ok"), sem("si_ok")
        mul_ok, ah_ok, act_ok, dn_ps = sem("mul_ok"), sem("ah_ok"), sem("act_ok"), sem("dn_ps")
        fin_ok, out_ok = sem("fin_ok"), sem("out_ok")

        ident = cn[:, K_ID:K_ID + P]
        ones = cn[:, K_ONES:K_ONES + P]
        blk = cn[:, K_BLK:K_BLK + P]
        LV = len(LEVELS)
        GROUPS = [(b, par_) for b in range(TB) for par_ in range(2)]

        def alone(eng):
            eng.sem_inc(passed, 1)

        block = ctx.enter_context(nc.Block())

        @block.sync
        def _(sp):
            def load(n, s):
                sp.wait_ge(lo_ok, n + 1)
                sp.dma_start(raw[:, s, :], ws[bass.ds(n, 1), :, :].rearrange("a p n -> (a p) n")).then_inc(landed[s], 16)

            for dst, src in ((cn[:, :], con), (parall[:, :, :], par), (cc[:, :], cT), (x[:, :, :], xT),
                             (posi[:, :], pos)):
                sp.dma_start(dst, src).then_inc(loaded, 16)
            with sp.Fori(0, (DEPTH * N_UNITS + AHEAD) // RING) as i:
                for s in range(RING):
                    load(i * RING + s, s)
            for n in range((DEPTH * N_UNITS + AHEAD) // RING * RING, DEPTH * N_UNITS + AHEAD):
                load(n, n % RING)
            sp.wait_ge(fin_ok, 1)
            sp.dma_start(out, sq).then_inc(out_ok, 16)
            sp.wait_ge(out_ok, 16)

        @block.gpsimd
        def _(pool):
            def piece(t, k, slot, free, signal=ada_in):
                pool.wait_ge(ada_used, free)
                alone(pool)
                pool.dma_start(ada[slot], wada[bass.ds(t * KT + k, 1), :, :].rearrange("a p n -> (a p) n")
                               ).then_inc(signal, 16)

            for k in range(KT):
                piece(0, k, k % 2, k + 1, ada_first[k % 2])
            with pool.Fori(0, DEPTH) as l:
                for k in range(KT):
                    piece(l * 3 + 1, k, 0, l * 16 + 8 + k + 2)
                pool.wait_ge(ada_used, l * 16 + 16 + 2)
                pool.wait_ge(sl_ok, l * N_SPLIT + S_LAT)
                alone(pool)
                pool.memset(fa[:, :, :], 1.0)
                pool.memset(fb[:, :, :], 1.0).then_inc(fl_one, 1)
                pool.wait_ge(fl_one, l + 1)
                pool.wait_ge(fl_cum, l + 1)
                alone(pool)
                pool.dma_start(fa[0:1, :, :].rearrange("p h t -> p (h t)"), fcum).then_inc(fl_dma, 16)
                pool.dma_start(fb[1:2, :, :].rearrange("p h t -> p (h t)"), fneg).then_inc(fl_dma, 16)
                for n in range(2 * H):
                    pool.wait_ge(adb_used, l * (2 * H) + n + 1)
                    alone(pool)
                    pool.dma_start(adb[n % 2], wada[bass.ds((l * 3 + 2) * KT + n // 2, 1), :, n % 2 * 1024:(n % 2 + 1) * 1024]
                                   .rearrange("a p n -> (a p) n")).then_inc(adb_in[n % 2], 16)
                pool.wait_ge(rk_mm, mm_at(l, "y"))
                for k in range(KT):
                    piece(l * 3 + 3, k, 0, l * 16 + 16 + k + 2)

        @block.scalar
        def _(a):
            def hi(l, u):
                a.wait_ge(landed[u % RING], l * (N_UNITS // RING * 16) + (u // RING + 1) * 16)
                a.wait_ge(unit_done, l * N_UNITS + u + 1)
                a.activation(wh[:, u % RING, :], raw[:, u % RING, :], ACT.Copy).then_inc(hi_ok, 1)

            def split(nth, dst, src):
                a.wait_ge(in_ok, nth)
                a.activation(dst, src, ACT.Copy).then_inc(sh_ok, 1)

            def root(nth, n):
                a.wait_ge(rec_ok, nth)
                a.activation(rs[:, 0:n, :], rs[:, 0:n, :], ACT.Sqrt).then_inc(rt_ok, 1)

            def square(k):
                a.activation(sq[:, k, :], x[:, k, :], ACT.Square).then_inc(sqx_ok, 1)

            a.wait_ge(loaded, 16 * 5)
            a.activation(csig[:, :], cc[:, :], ACT.Sigmoid).then_inc(csig_ok, 1)
            a.wait_ge(trig_r, 1)
            a.activation(trig[:, :], trig[:, :], ACT.Sin).then_inc(trig_ok, 1)
            for k in range(KT):
                square(k)
            root(1, 1)
            for u in range(AHEAD):
                hi(0, u)
            with a.Fori(0, DEPTH) as l:
                def norm(h0, sh_col):
                    for k in range(KT):
                        a.wait_ge(t_norm, l * (2 * KT) + (h0 > 0) * KT + k + 1)
                        a.activation(hh[:, k, :], sq[:, k, :], ACT.Identity, bias=mod[:, sh_col + k:sh_col + k + 1]
                                     ).then_inc(hh_ok, 1)

                def project(u):
                    a.wait_ge(unit_done, done(l, u))
                    a.activation(proj[:, u if u < U_LORA else u - 2, 1:SEQ + 1], ps[:, u % RING, 0:SEQ], ACT.Copy).then_inc(a_free, 1)

                norm(H_N1, 0)
                with a.Fori(0, 5) as i:
                    for s in range(RING):
                        a.wait_ge(landed[(s + 2) % RING], (l * (N_UNITS // RING) + i + (s + 2) // RING + 1) * 16)
                        a.wait_ge(unit_done, l * N_UNITS + i * RING + s + 3)
                        a.activation(wh[:, (s + 2) % RING, :], raw[:, (s + 2) % RING, :], ACT.Copy).then_inc(hi_ok, 1)
                        a.wait_ge(unit_done, done(l, i * RING + s))
                        a.activation(proj[:, bass.ds(i * RING + s, 1), 1:SEQ + 1], ps[:, s, 0:SEQ], ACT.Copy).then_inc(a_free, 1)
                hi(l, 17)
                a.wait_ge(shift_ok, l * 5 + 1)
                a.activation(tw[0:64, 0, :], proj[0:64, T_WA, 1:], ACT.Tanh)
                a.activation(tw[64:128, 0, :], proj[64:128, T_WA, 1:], ACT.Copy)
                a.activation(tw[:, 1, :], proj[:, T_GL, 1:], ACT.Sigmoid).then_inc(in_ok, 1)
                split(l * 3 + 1, sh[:, 0:2, :], tw)
                a.activation(sh[:, 2, :], proj[:, T_MIX, 1:], ACT.Copy).then_inc(sh_ok, 1)
                project(15)
                hi(l, 18)
                project(16)
                a.wait_ge(shift_ok, l * 5 + 5)
                for m in range(4):
                    a.activation(kkn[:, m, :], proj[:, T_K + m, 1:], ACT.Copy, scale=pr[:, C_KK + m:C_KK + m + 1])
                for m in range(4):
                    last = a.activation(sqk[:, m, :], proj[:, T_K + m, 1:], ACT.Square, scale=pr[:, C_KK + m:C_KK + m + 1])
                last.then_inc(kq_ok, 1)
                for u in (17, 18):
                    hi(l, u + 2)
                    project(u)
                hi(l, 21)
                a.wait_ge(unit_done, done(l, U_LORA))
                for m in range(4):
                    a.activation(lgd[:, m, :], span(3)[:, m, :], ACT.Sigmoid, bias=pr[:, C_W0 + m:C_W0 + m + 1]).then_inc(lora_ev, 1)
                a.activation(gg[:, 2:4, :], two(U_LORA % RING), ACT.Copy).then_inc(a_free, 1)
                hi(l, 22)
                for m in range(4):
                    a.activation(aa[:, m, :], span(5)[:, m, :], ACT.Sigmoid, bias=pr[:, C_A0 + m:C_A0 + m + 1]).then_inc(lora_ev, 1)
                a.activation(gg[:, 0:2, :], two(7), ACT.Copy).then_inc(lora_ev, 1)
                a.wait_ge(unit_done, done(l, U_LORA + 1))
                for m in range(2):
                    last = a.activation(tmp[:, m, :], two((U_LORA + 1) % RING)[:, m, :], ACT.Sigmoid, bias=pr[:, C_V0 + m:C_V0 + m + 1])
                last.then_inc(a_free, 1)
                for m in range(2, 4):
                    last = a.activation(tmp[:, m, :], two(3)[:, m - 2, :], ACT.Sigmoid, bias=pr[:, C_V0 + m:C_V0 + m + 1])
                last.then_inc(lora_ev, 1)
                a.wait_ge(lora_ev, l * 10 + 8)
                for m in range(4):
                    last = a.activation(fac[:, m, :], aa[:, m, :], ACT.Identity, bias=ka1[:, m:m + 1], scale=pr[:, C_KA + m:C_KA + m + 1])
                last.then_inc(fac_ok, 1)
                hi(l, 23)
                project(21)
                a.wait_ge(cum_ok, l * 2 + 1)
                a.activation(ar[:, :, :, 1, :], cum.rearrange("p m (b t) -> p m b t", b=TB), ACT.Exp, scale=-RSQ_E)
                a.activation(kap, cum, ACT.Exp, scale=RSQ_E)
                hi(l, 24)
                project(22)
                a.activation(ar[:, :, :, 0, :], lgd.rearrange("p m (b t) -> p m b t", b=TB), ACT.Exp, scale=-RSQ_E).then_inc(exp_ok, 1)
                hi(l, 25)
                project(23)
                root(l * N_NORM + 2, 2)
                hi(l, 26)
                project(24)
                hi(l, 27)
                project(25)
                a.wait_ge(cum_ok, l * 2 + 2)
                a.activation(tmp, tmp, ACT.Sqrt).then_inc(exp_ok, 1)
                split(l * 3 + 2, sh[:, :, :], lat)
                for u in (26, 27, 28):
                    hi(l, u + 2)
                    project(u)
                for e in range(2):
                    hi(l, 31 + 2 * e)
                    a.wait_ge(unit_done, done(l, U_FV + 2 * e + 1))
                    for b in range(TB):
                        last = a.activation(vf[:, b, e * 256:(e + 1) * 256], ps[:, FV_BANKS[e][b], 0:256], ACT.Copy)
                    last.then_inc(a_free, 1)
                    hi(l, 32 + 2 * e)
                a.wait_ge(fl_in, l + 1)
                a.activation(ft, ft, ACT.Exp).then_inc(fl_exp, 1)
                a.wait_ge(fl_exp, l * 2 + 1)
                a.activation(ft, ft, ACT.Ln, bias=1.0).then_inc(fl_exp, 1)
                for e in range(2):
                    hi(l, 35 + e)
                    a.wait_ge(unit_done, done(l, U_QUP + e))
                    a.activation(qh[0:64, 4 * e:4 * e + 4, :], span(5 - 2 * e)[0:64], ACT.Copy).then_inc(up_ok, 1)
                hi(l, 37)
                a.wait_ge(unit_done, done(l, U_KUP))
                kk = kh.rearrange("p (m e) t -> p m e t", e=2)
                for e in range(2):
                    a.activation(kk[0:64, :, e, :], span(0)[64 * e:64 * e + 64], ACT.Copy).then_inc(up_ok, 1)
                hi(l, 38)
                a.wait_ge(unit_done, done(l, U_VUP))
                a.activation(vm[:, 0, :], ps[:, 2, :], ACT.Copy)
                a.activation(vm[:, 1, :], ps[:, 7, :], ACT.Copy).then_inc(up_ok, 1)
                for n in range(2 * H + 2):
                    if n < 2 * H:
                        scale = HD ** -0.5 if n < H else (NOPE + ROPE) ** -0.5
                        a.wait_ge(s_ok, l * (2 * H) + n + 1)
                        if n >= 3:
                            a.wait_ge(pt_ps, l * (2 * H) + n - 2)
                        a.activation(pp[:, n % 3, 0:128], sc[:, n % 3, 0:128], ACT.Exp, bias=nb[:, n % 3, 0:1],
                                     scale=scale, accum_out=den[:, n % 3, 0:1])
                        a.activation(pp[:, n % 3, 128:384], sc[:, n % 3, 128:384], ACT.Exp, bias=nb[:, n % 3, 1:2],
                                     scale=scale, accum_out=den[:, n % 3, 1:2]).then_inc(p_ok, 1)
                    if 1 <= n <= 2 * H:
                        a.wait_ge(pt_ps, l * (2 * H) + n)
                        if n >= 3:
                            a.wait_ge(o_ps, l * (2 * H) + n - 2)
                        a.activation(pT[:, (n - 1) % 2, :], ps[:, 3 + (n - 1) % 2, 0:384], ACT.Copy).then_inc(pt_ok, 1)
                    if n >= 3 and n % 2:
                        a.wait_ge(o_ps, l * (2 * H) + n - 1)
                        a.activation(y[:, 3 + n // 2, :], ps[:, 5 + (n // 2 - 1) % 2, 0:SEQ], ACT.Copy).then_inc(o_ok, 1)
                a.wait_ge(o_ok, l * H + H)

                def gated(u, dst):
                    a.wait_ge(unit_done, done(l, u))
                    a.activation(dst, ps[:, u % RING, 0:SEQ], ACT.Sigmoid).then_inc(a_free, 1)

                def gb(u, last_merged=None):
                    e = (u - U_GB) % 3 if u < U_GR else u - U_GL
                    if e < 2:
                        if u >= U_GB + 3:
                            a.wait_ge(v_free, v_at(l, last_merged or u - e - 1))
                        gated(u, gate[:, e, :])

                for g, (b, par_) in enumerate(GROUPS):
                    u0 = U_GB + 6 * g

                    if par_ == 0:
                        a.wait_ge(rk_mm, mm_at(l, f"tr{b}"))
                        a.activation(toks[:, 0:3, :], ps[:, 3:6, :], ACT.Copy).then_inc(tra_ok, 1)
                        a.wait_ge(unit_done, done(l, u0 - 1))
                        a.activation(sh[:, :, :], y[:, 4 + 2 * g:8 + 2 * g, :], ACT.Copy).then_inc(sh_ok, 1)
                    hi(l, u0 + 2)
                    gb(u0)
                    for i in range(LV):
                        a.wait_ge(rk_mm, mm_at(l, f"X{b}{par_}{i}"))
                        a.activation(xx, four(7), ACT.Copy).then_inc(rk_ev, 1)
                        if g < 3 or i < 2:
                            hi(l, u0 + i + 3)
                            gb(u0 + i + 1)
                    a.wait_ge(rk_mm, mm_at(l, f"WU{b}{par_}"))
                    a.activation(wu, four(7), ACT.Copy).then_inc(rk_ev, 1)
                for u in range(U_GR, U_BR):
                    hi(l, u + 2)
                    if u == U_BR - 1:
                        a.wait_ge(unit_done, done(l, U_GL + 2))
                        split(l * 3 + 3, sh[:, :, :], y[:, 0:4, :])
                    if u == U_GL + 2:
                        a.wait_ge(rk_ev, ev_at(l, "var"))
                        a.activation(tmp, tmp, ACT.Sqrt).then_inc(exp_ok, 1)
                    if U_GL <= u < U_GL + 3:
                        gb(u, U_GR - 1)
                    else:
                        t = gr_tile(u)
                        gated(u, gr[:, t, :])
                for i in range(4):
                    hi(l, U_BR + i + 2)
                    a.wait_ge(mg_ok, l * 4 + i + 1)
                    a.activation(hh[:, 2 * i:2 * i + 2, :], merged[:, 2 * i:2 * i + 2, :], ACT.Copy).then_inc(hh_ok, 1)
                for t in range(KT):
                    hi(l, U_WO + t + 2)
                for k in range(KT):
                    a.wait_ge(v_free, v_at(l, U_WO + k))
                    square(k)
                root(l * N_NORM + 3, 1)
                norm(H_N2, 24)

                def conv(j, r):
                    a.wait_ge(unit_done, l * N_UNITS + RING + (up_unit(j) if isinstance(j, int) else U_FF + 4 + 3 * (j - 2)) + 2)
                    for e in range(2):
                        last = a.activation(cg[:, r, e, :], two(r)[:, e, :], ACT.Identity,
                                            bias=pr[:, bass.ds(C_CB + e * FT + j, 1)], scale=pr[:, bass.ds(C_CW + (4 + e) * FT + j, 1)])
                    last.then_inc(cv_ok, 1)

                def silu(j, r):
                    a.wait_ge(cv2_ok, l * FT + j + 1)
                    a.activation(sg[:, r, :], cg[:, r, 0, :], ACT.Silu).then_inc(si_ok, 1)

                def act_hi(j, r):
                    a.wait_ge(mul_ok, l * FT + j + 1)
                    a.activation(sh[:, r, :], sg[:, r, :], ACT.Copy).then_inc(ah_ok, 1)

                for j in range(2):
                    hi(l, U_FF + 2 * j + 2)
                    hi(l, U_FF + 2 * j + 3)
                    if j:
                        act_hi(0, 0)
                    conv(j, j)
                    silu(j, j)
                with a.Fori(0, (FT - 2) // 4) as i:
                    for o in range(4):
                        j, r = 2 + 4 * i + o, (2 + o) % 4

                        def hi_ff(e):
                            s = (U_FF + 3 * o + e) % RING
                            a.wait_ge(landed[s], (l * (N_UNITS // RING) + i * 4 + (U_FF + 6 + 3 * o + e) // RING + 1) * 16)
                            a.wait_ge(unit_done, l * N_UNITS + i * 12 + U_FF + 6 + 3 * o + e + 1)
                            a.activation(wh[:, s, :], raw[:, s, :], ACT.Copy).then_inc(hi_ok, 1)

                        hi_ff(0)
                        hi_ff(1)
                        act_hi(j - 1, (r + 3) % 4)
                        conv(j, r)
                        hi_ff(2)
                        silu(j, r)
                act_hi(FT - 1, (FT - 1) % 4)
                hi(l, N_UNITS)
                hi(l, N_UNITS + 1)
                for k in range(KT):
                    a.wait_ge(x_ok, l * KT + k + 1)
                    square(k)
                root(l * N_NORM + 4, 1)

        @block.vector
        def _(v):
            count = [0]
            base = [0]

            def step(ins):
                ins.then_inc(dv, 1)
                count[0] += 1
                v.wait_ge(dv, base[0] + count[0])

            def lo(l, u):
                v.wait_ge(hi_ok, l * N_UNITS + u + 1)
                v.tensor_tensor(wl[:, u % RING, :], raw[:, u % RING, :], wh[:, u % RING, :], ALU.subtract).then_inc(lo_ok, 1)

            def piece(turn, k, slot=0, first=None):
                if isinstance(turn, int):
                    v.wait_ge(ada_first[slot], (k // 2 + 1) * 16)
                else:
                    v.wait_ge(ada_in, turn * (KT * 16) + (k + 1 - KT) * 16)
                if first if first is not None else (isinstance(k, int) and k == 0):
                    v.tensor_scalar(acc, ada[slot], cc[:, 0:1], None, ALU.mult).then_inc(ada_used, 1)
                else:
                    v.wait_ge(ada_used, turn * KT + k + 2)
                    v.scalar_tensor_tensor(acc, ada[slot], cc[:, bass.ds(k, 1)] if not isinstance(k, int) else cc[:, k:k + 1], acc,
                                           ALU.mult, ALU.add).then_inc(ada_used, 1)

            def mod_third(t, bank, dst, bias):
                v.wait_ge(mod_ps, t + 1)
                v.tensor_tensor(dst, ps[:, bank, 0:16], bias, ALU.add).then_inc(mod_ok, 1)
                v.wait_ge(mod_ok, t + 1)

            def gains(sc_col, g):
                step(v.tensor_scalar(gain[:, :], mod[:, sc_col:sc_col + KT], 1.0, None, ALU.add))
                step(v.tensor_tensor(gain[:, :], gain[:, :], g, ALU.mult))

            def inv_square(nth, bank, n, width):
                v.wait_ge(ss_ps, nth)
                step(v.tensor_scalar(rs[:, 0:n, :], two(bank)[:, 0:n, :], 1.0 / width, 1e-6, ALU.mult, ALU.add))
                v.reciprocal(rs[:, 0:n, :], rs[:, 0:n, :]).then_inc(rec_ok, 1)

            v.sem_inc(unit_done, RING)
            v.sem_inc(lo_ok, RING)
            v.sem_inc(a_free, RING)
            v.sem_inc(ada_used, 2)
            v.sem_inc(adb_used, 2)
            v.sem_inc(taps_ok, 4)
            v.memset(v1st[:, :, :], 0.0)
            v.memset(proj[:, :, 0:1], 0.0)
            v.wait_ge(loaded, 16 * 5)
            v.wait_ge(csig_ok, 1)
            step(v.tensor_tensor(cc[:, :], cc[:, :], csig[:, :], ALU.mult))
            step(v.tensor_copy(sq[:, 0, :], posi[:, :]))
            step(v.tensor_scalar(sq[:, 0, :], sq[:, 0, :], cn[:, K_TRIG:K_TRIG + 1], None, ALU.mult))
            step(v.tensor_scalar(sq[:, 1, :], sq[:, 0, :], 1.0 / TWO_PI, cn[:, K_TRIG + 1:K_TRIG + 2], ALU.mult, ALU.add))
            step(v.tensor_scalar(sq[:, 2, :], sq[:, 1, :], MAGIC, None, ALU.add))
            step(v.tensor_scalar(sq[:, 1, :], sq[:, 2, :], MAGIC, None, ALU.subtract))
            for c in (PI2_A, PI2_B, PI2_C):
                step(v.scalar_tensor_tensor(sq[:, 0, :], sq[:, 1, :], -c, sq[:, 0, :], ALU.mult, ALU.add))
            step(v.tensor_scalar(sq[:, 0, :], sq[:, 0, :], cn[:, K_TRIG + 2:K_TRIG + 3], None, ALU.add))
            v.tensor_scalar(trig[:, :], sq[:, 0, :], -3.1415925, 3.1415925, ALU.max, ALU.min).then_inc(trig_r, 1)
            v.wait_ge(trig_ok, 1)
            step(v.tensor_scalar(trig[:, :], trig[:, :], cn[:, K_TRIG + 3:K_TRIG + 4], None, ALU.mult))
            for k in range(KT):
                if k == KT // 2:
                    inv_square(1, 3, 1, D_MODEL)
                piece(0, k, k % 2)
            for u in range(AHEAD):
                lo(0, u)
            mod_third(0, 2, mod[:, 0:16], parall[:, 0, C_BADA:C_BADA + 16])
            gains(8, parall[:, 0, C_N1:C_N1 + KT])
            pre = count[0]
            count[0] = 0

            with v.Fori(0, DEPTH) as l:
                base[0] = l * N_DV + pre

                def norm(nth, sh_col, h0):
                    v.wait_ge(rt_ok, l * N_NORM + nth)
                    for k in range(KT + 2):
                        if k < KT:
                            v.scalar_tensor_tensor(sq[:, k, :], x[:, k, :], gain[:, k:k + 1], rs[:, 0, :], ALU.mult, ALU.mult
                                                   ).then_inc(t_norm, 1)
                        if k >= 2:
                            v.wait_ge(hh_ok, l * N_H + h0 + k - 1)
                            v.scalar_tensor_tensor(hl[:, k - 2, :], sq[:, k - 2, :], mod[:, sh_col + k - 2:sh_col + k - 1],
                                                   hh[:, k - 2, :], ALU.add, ALU.subtract).then_inc(h_ok, 1)

                def sub_split(n, dst, src, leading):
                    v.wait_ge(sh_ok, n)
                    v.tensor_tensor(dst, src, leading, ALU.subtract).then_inc(sl_ok, 1)

                step(v.tensor_copy(pr[:, :], parall[:, bass.ds(l, 1), :]))
                v.tensor_scalar(ka1[:, :], pr[:, C_KA:C_KA + 4], -1.0, 1.0, ALU.mult, ALU.add)
                norm(1, 0, H_N1)
                piece(l * 2 + 1, 0)

                per = 1
                outer = base[0]
                with v.Fori(0, 5) as i:
                    base[0] = outer + i * per
                    start = count[0]
                    for s in range(RING):
                        t = (s + 2) % RING
                        v.wait_ge(hi_ok, l * N_UNITS + i * RING + s + 3)
                        v.tensor_tensor(wl[:, t, :], raw[:, t, :], wh[:, t, :], ALU.subtract).then_inc(lo_ok, 1)
                    piece(l * 2 + 1, i + 1, first=False)
                    v.wait_ge(a_free, l * N_A + i * RING + 3 + RING)
                    step(v.tensor_tensor(shd, proj[:, bass.ds(i * 3, 3), 0:SEQ], proj[:, bass.ds(i * 3, 3), 1:SEQ + 1], ALU.subtract))
                    for t in range(3):
                        ins = v.scalar_tensor_tensor(proj[:, bass.ds(i * 3 + t, 1), 1:SEQ + 1], shd[:, t:t + 1, :],
                                                     pr[:, bass.ds(C_MU + i * 3 + t, 1)],
                                                     proj[:, bass.ds(i * 3 + t, 1), 1:SEQ + 1], ALU.mult, ALU.add)
                    ins.then_inc(shift_ok, 1)
                    assert count[0] - start == per
                base[0] = outer
                count[0] += 4 * per
                rr, kx, vx = (proj[:, t:t + 4, 1:SEQ + 1] for t in (T_R, T_K, T_V))
                lo(l, 17)
                v.wait_ge(sh_ok, l * (N_SPLIT + 1) + 2)
                v.tensor_tensor(sl[:, 0:2, :], tw, sh[:, 0:2, :], ALU.subtract)
                v.tensor_tensor(sl[:, 2, :], proj[:, T_MIX, 1:], sh[:, 2, :], ALU.subtract).then_inc(sl_ok, 1)
                lo(l, 18)
                piece(l * 2 + 1, 6)
                lo(l, 19)
                piece(l * 2 + 1, 7)
                lo(l, 20)
                v.wait_ge(a_free, a_at(l, 18))
                v.tensor_tensor(sq[:, 0:4, :], proj[:, T_MQ:T_MQ + 4, 1:], proj[:, T_MQ:T_MQ + 4, 1:], ALU.mult).then_inc(sq_ok, 1)
                lo(l, 21)
                lo(l, 22)
                for m in range(4):
                    v.wait_ge(lora_ev, l * 10 + m + 1)
                    ins = v.tensor_tensor_scan(cum[:, m, :], cn[:, K_RST:K_RST + SEQ], lgd[:, m, :], 0.0, ALU.mult, ALU.add)
                step(ins)
                v.tensor_tensor(lgd, cum, lgd, ALU.subtract).then_inc(cum_ok, 1)
                lo(l, 23)
                step(v.tensor_tensor(vt, v1st[:, :, :], vx, ALU.subtract))
                v.wait_ge(lora_ev, l * 10 + 10)
                step(v.scalar_tensor_tensor(vt, vt, pr[:, C_FLAG:C_FLAG + 1], tmp, ALU.mult, ALU.mult))
                step(v.tensor_tensor(vx, vx, vt, ALU.add))
                lo(l, 24)
                v.scalar_tensor_tensor(v1st[:, :, :], vx, pr[:, C_FLAG + 1:C_FLAG + 2], v1st[:, :, :], ALU.mult, ALU.add)
                v.wait_ge(fac_ok, l + 1)
                step(v.tensor_tensor(kx, kx, fac, ALU.mult))
                v.wait_ge(exp_ok, l * 3 + 1)
                for m in range(4):
                    ins = v.scalar_tensor_tensor(bon[:, m, :], rr[:, m, :], pr[:, C_RK + m:C_RK + m + 1], kx[:, m, :], ALU.mult, ALU.mult)
                ins.then_inc(rk_ev, 1)
                lo(l, 25)
                inv_square(l * N_NORM + 2, 7, 2, 256)
                lo(l, 26)
                v.wait_ge(rk_mm, mm_at(l, "ksq"))
                step(v.tensor_scalar(tmp, span(5), 1e-24, None, ALU.max))
                v.reciprocal(tmp[:, 0:2, :], tmp[:, 0:2, :])
                lo(l, 27)
                v.reciprocal(tmp[:, 2:4, :], tmp[:, 2:4, :]).then_inc(cum_ok, 1)
                v.wait_ge(rt_ok, l * N_NORM + 2)
                for t in range(4):
                    ins = v.scalar_tensor_tensor(lat[:, t, :], proj[:, T_MQ + t, 1:], pr[:, C_MQ + t:C_MQ + t + 1], rs[:, t // 2, :],
                                                 ALU.mult, ALU.mult)
                ins.then_inc(in_ok, 1)
                for b in range(TB):
                    v.tensor_copy(pc[:, :, 2 * b:2 * b + 2], ar[:, :, b, 1, :].rearrange("p m (c t) -> p m c t", c=2)[:, :, :, CHUNK - 1])
                v.wait_ge(rk_mm, mm_at(l, "bonus"))
                v.tensor_tensor(bon, span(3), vx, ALU.mult).then_inc(rk_ev, 1)
                lo(l, 28)
                sub_split(l * (N_SPLIT + 1) + 3, sl[:, :, :], lat, sh[:, :, :])
                v.wait_ge(exp_ok, l * 3 + 2)
                step(v.tensor_tensor(kkn, kkn, tmp, ALU.mult))
                lo(l, 29)
                step(v.tensor_tensor(bet, kkn, aa, ALU.mult))
                v.tensor_tensor(bet, bet, kap, ALU.mult)
                step(v.tensor_tensor(kap, kx, kap, ALU.mult))
                lo(l, 30)
                v.tensor_tensor(ar[:, :, :, 0, :], ar[:, :, :, 0, :], kkn.rearrange("p m (b t) -> p m b t", b=TB), ALU.mult)
                step(v.tensor_scalar(flog, proj[0:8, T_MIX, 1:SEQ + 1], pr[0:8, C_MIX:C_MIX + 1], None, ALU.add))
                step(v.tensor_scalar(fneg, flog, -1.0, None, ALU.mult))
                v.tensor_tensor(ft, flog, fneg, ALU.min).then_inc(fl_in, 1)
                v.wait_ge(fl_in, l + 1)
                step(v.tensor_scalar(flog, flog, 0.0, None, ALU.min))
                lo(l, 31)
                lo(l, 32)
                mod_third(l * 3 + 1, 7, mod[:, 16:32], pr[:, C_BADA + 16:C_BADA + 32])
                v.tensor_tensor(ar[:, :, :, 1, :], ar[:, :, :, 1, :], rr.rearrange("p m (b t) -> p m b t", b=TB), ALU.mult
                                ).then_inc(rk_ev, 1)
                v.wait_ge(rk_ev, ev_at(l, "rho"))
                lo(l, 33)
                cos = trig[64:96, :].rearrange("p (a t) -> p a t", a=1)
                sin = trig[96:128, :].rearrange("p (a t) -> p a t", a=1)
                v.tensor_tensor(rtmp[:, 0, :], proj[96:128, T_MIX, 1:SEQ + 1], trig[96:128, :], ALU.mult)
                step(v.tensor_tensor(rtmp[:, 1, :], proj[64:96, T_MIX, 1:SEQ + 1], trig[64:96, :], ALU.mult))
                step(v.tensor_tensor(rtmp[:, 0, :], rtmp[:, 0, :], rtmp[:, 1, :], ALU.add))
                step(v.tensor_copy(kh[64:96, :, :], rtmp[:, 0:1, :].broadcast_to([32, H, SEQ])))
                lo(l, 34)
                v.wait_ge(fl_exp, l * 2 + 2)
                step(v.tensor_tensor(flog, flog, ft, ALU.subtract))
                step(v.tensor_tensor_scan(ft, cn[0:8, K_ONES:K_ONES + SEQ], flog, 0.0, ALU.mult, ALU.add))
                v.tensor_scalar(fcum, ft, 8.0, None, ALU.mult)
                v.tensor_scalar(fneg, ft, -8.0, None, ALU.mult).then_inc(fl_cum, 1)
                for e in range(2):
                    lo(l, 35 + e)
                    v.wait_ge(up_ok, l * 5 + e + 1)
                    o = span(5 - 2 * e)
                    v.tensor_tensor(rtmp[:, 4 * e:4 * e + 4, :], o[96:128], sin.broadcast_to([32, 4, SEQ]), ALU.mult)
                    step(v.tensor_tensor(qh[64:96, 4 * e:4 * e + 4, :], o[64:96], cos.broadcast_to([32, 4, SEQ]), ALU.mult))
                    v.tensor_tensor(qh[64:96, 4 * e:4 * e + 4, :], qh[64:96, 4 * e:4 * e + 4, :], rtmp[:, 4 * e:4 * e + 4, :],
                                    ALU.add).then_inc(rope_ok, 1)
                lo(l, 37)
                lo(l, 38)

                def half_piece(p):
                    v.wait_ge(adb_in[p % 2], l * (H * 16) + (p // 2 + 1) * 16)
                    part = acc2[:, p % 2 * 1024:(p % 2 + 1) * 1024]
                    if p < 2:
                        v.tensor_scalar(part, adb[p % 2], cc[:, 0:1], None, ALU.mult).then_inc(adb_used, 1)
                    else:
                        v.wait_ge(adb_used, l * (2 * H) + p + 1)
                        v.scalar_tensor_tensor(part, adb[p % 2], cc[:, p // 2:p // 2 + 1], part, ALU.mult, ALU.add
                                               ).then_inc(adb_used, 1)

                for n in range(2 * H + 1):
                    if n < 2 * H:
                        scale = HD ** -0.5 if n < H else (NOPE + ROPE) ** -0.5
                        v.wait_ge(s_ps, l * (2 * H) + n + 1)
                        if n >= 3:
                            v.wait_ge(p_ok, l * (2 * H) + n - 2)
                        alone(v)
                        v.tensor_tensor_reduce(sc[:, n % 3, 0:128], ps[:, n % 3, 0:128], cn[:, K_CAUS + 128:K_CAUS + 256],
                                               1.0, NEG, ALU.add, ALU.max, mx[:, n % 3, 0:1])
                        step(v.tensor_tensor_reduce(sc[:, n % 3, 128:384], ps[:, n % 3, 128:384], cn[:, K_CAUS:K_CAUS + 256],
                                                    1.0, NEG, ALU.add, ALU.max, mx[:, n % 3, 1:2]))
                        v.tensor_scalar(nb[:, n % 3, :], mx[:, n % 3, :], -scale, None, ALU.mult).then_inc(s_ok, 1)
                    if n < len(PIECES):
                        half_piece(sum(PIECES[:n]))
                    if n >= 1:
                        r = (n - 1) % 3
                        v.wait_ge(p_ok, l * (2 * H) + n)
                        step(v.reciprocal(rd[:, r, :], den[:, r, :]))
                        v.tensor_scalar(pp[:, r, 0:128], pp[:, r, 0:128], rd[:, r, 0:1], None, ALU.mult)
                        v.tensor_scalar(pp[:, r, 128:384], pp[:, r, 128:384], rd[:, r, 1:2], None, ALU.mult).then_inc(pn_ok, 1)
                    if n < len(PIECES) and PIECES[n] == 2:
                        half_piece(sum(PIECES[:n]) + 1)
                mod_third(l * 3 + 2, 7, mod[:, 32:48], pr[:, C_BADA + 32:C_BADA + 48])
                gains(32, pr[:, C_N2:C_N2 + KT])

                def evac(ins, name):
                    ins.then_inc(rk_ev, 1)
                    v.wait_ge(rk_ev, ev_at(l, name))

                def mask(at, n=4):
                    return cn[:, at:at + P].rearrange("p (a t) -> p a t", a=1).broadcast_to([P, n, P])

                def merge(u, tiles, gates, first):
                    v.wait_ge(unit_done, done(l, u))
                    src = two(u % RING)
                    if first:
                        v.tensor_tensor(merged[:, tiles, :], src, gates, ALU.mult).then_inc(v_free, 1)
                    else:
                        step(v.tensor_tensor(gates, src, gates, ALU.mult))
                        v.tensor_tensor(merged[:, tiles, :], merged[:, tiles, :], gates, ALU.add).then_inc(v_free, 1)

                def merge_gb(u):
                    i = (u - U_GB) // 3 % 4 if u < U_GR else 3
                    v.wait_ge(a_free, a_at(l, u - 1))
                    merge(u, slice(2 * i, 2 * i + 2), gate, u < U_GB + 12)

                for g, (b, par_) in enumerate(GROUPS):
                    u0 = U_GB + 6 * g
                    name = f"{b}{par_}"
                    if g % 2 == 0:
                        v.wait_ge(rk_mm, mm_at(l, f"tr{b}"))
                        v.tensor_copy(toks[:, 3, :], ps[:, 6, :])
                        evac(v.tensor_scalar(v0n[:, :, 64:128], ps[:, 6, :].rearrange("p (h c) -> p h c", h=H), -1.0, None, ALU.mult),
                             f"tr{b}")
                    v.wait_ge(rk_mm, mm_at(l, f"N{name}"))
                    step(v.tensor_tensor(tt, four(7), mask(K_N2), ALU.mult))
                    v.tensor_tensor(tt, tt, mask(K_ID), ALU.add)
                    if g == 0:
                        v.memset(v0n[:, :, 0:64], 0.0)
                    v.wait_ge(rk_mm, mm_at(l, f"S{name}"))
                    step(v.tensor_tensor(lbT, span(5)[:, :, 0:128], mask(K_MS), ALU.mult))
                    evac(v.tensor_tensor(loT, lbT, mask(K_OFF), ALU.mult), f"S{name}")
                    step(v.tensor_tensor(ttT, lbT, mask(K_N2T), ALU.mult))
                    v.tensor_tensor(ttT, ttT, mask(K_ID), ALU.add)
                    v.tensor_tensor(lakT, span(3)[:, :, 0:128], mask(K_MS), ALU.mult)
                    v.tensor_tensor(mrkT, span(3)[:, :, 128:256], mask(K_MI), ALU.mult)
                    v.tensor_tensor(mrbT, span(5)[:, :, 128:256], mask(K_MI), ALU.mult).then_inc(m_ok, 1)
                    lo(l, u0 + 2)
                    if par_ == 0:
                        sub_split(l * (N_SPLIT + 1) + 4 + g // 2, sl[:, :, :], y[:, 4 + 2 * g:8 + 2 * g, :], sh[:, :, :])
                    for i in range(LV):
                        last = i == LV - 1
                        v.wait_ge(rk_mm, mm_at(l, f"X{name}{i}"))
                        if not last:
                            v.tensor_tensor(loT, lbT, mask(K_OFF + (i + 1) * P), ALU.mult)
                        if g < 3 or i < 2:
                            lo(l, u0 + i + 3)
                        if not last:
                            v.wait_ge(rk_mm, mm_at(l, f"T{name}{i}"))
                            v.tensor_tensor(tt, tt, four(5), ALU.subtract).then_inc(t_ok, 1)
                        v.wait_ge(rk_mm, mm_at(l, f"TT{name}{i}"))
                        v.tensor_tensor(ttT, ttT, four(4), ALU.subtract).then_inc(rk_ev, 1)
                        if i == 0:
                            if par_ == 0:
                                v.wait_ge(tra_ok, l * TB + b + 1)
                            v.tensor_copy(rhs[:, :, 0:64], toks[:, 0, :].rearrange("p (m e c) -> p m e c", m=4, e=2)[:, :, par_, :])
                            v.tensor_copy(rhs[:, :, 64:128], ps[:, 6, 0:256].rearrange("p (m c) -> p m c", m=4)).then_inc(t_ok, 1)
                        if i == 1 or i == 4 and g < 3:
                            merge_gb(u0 + i + 1)
                    v.wait_ge(rk_mm, mm_at(l, f"ZG{name}"))
                    p0 = 64 * par_
                    rows = slice(p0, p0 + 64)
                    z = four(3)
                    t0 = CHUNK if b == 0 else 0
                    v.tensor_tensor(zT[rows, :, b * P + t0 - CHUNK:(b + 1) * P - CHUNK], ar[rows, :, b, 1, t0:P], z[0:64, :, t0:P], ALU.subtract)
                    ins = v.tensor_scalar(y[rows, 0:4, b * P:(b + 1) * P], z[64:128], -1.0, None, ALU.mult)
                    for c in range(2):
                        q = 2 * b + c
                        o = ps[rows, 4 + c, :].rearrange("p (e m c) -> p e m c", e=2, m=4)
                        if q < NCH - 1:
                            ins = v.tensor_tensor(hP[rows, q, :, :], o[:, 0, :, :], pc[rows, :, q:q + 1].broadcast_to([64, 4, 64]), ALU.mult)
                        if 0 < q < NCH - 1:
                            ins = v.tensor_tensor(gT[rows, q - 1, :, :], cn[rows, K_ID + p0:K_ID + p0 + 64]
                                                  .rearrange("p (a t) -> p a t", a=1).broadcast_to([64, 4, 64]), o[:, 1, :, :], ALU.subtract)
                    evac(ins, f"ZG{name}")
                evac(v.tensor_scalar(st[:, 0, :, :], hP[:, 0, :, :], -1.0, None, ALU.mult), "st0")
                lo(l, U_GR + 2)
                for q in range(1, NCH - 1):
                    v.wait_ge(rk_mm, mm_at(l, f"st{q}"))
                    for p0 in (0, 64):
                        ins = v.tensor_tensor(stn[p0:p0 + 64], ps[p0:p0 + 64, 3 + p0 // 64, 0:256].rearrange("p (m c) -> p m c", m=4),
                                              pc[p0:p0 + 64, :, q:q + 1].broadcast_to([64, 4, 64]), ALU.mult)
                    step(ins)
                    evac(v.tensor_tensor(st[:, q, :, :], stn, hP[:, q, :, :], ALU.subtract), f"st{q}")
                    lo(l, U_GR + 2 + q)
                v.memset(proj[:, T_R:T_R + 3, 0:1], 0.0)
                ya = y[:, 0:4, :]
                v.wait_ge(rk_mm, mm_at(l, "y"))
                for p0 in (0, 64):
                    ins = v.tensor_tensor(ya[p0:p0 + 64, :, CHUNK:], ya[p0:p0 + 64, :, CHUNK:],
                                          span(3 + p0 // 32)[p0:p0 + 64, :, CHUNK:], ALU.add)
                evac(ins, "y")
                lo(l, U_GR + 5)
                v.wait_ge(rk_mm, mm_at(l, "mean"))
                step(v.scalar_tensor_tensor(ya, span(3), -1.0 / HD, ya, ALU.mult, ALU.add))
                evac(v.tensor_tensor(tmp, ya, ya, ALU.mult), "mean")
                lo(l, U_GR + 6)
                v.wait_ge(rk_mm, mm_at(l, "var"))
                step(v.tensor_scalar(tmp, span(5), 1.0 / HD, 64e-5, ALU.mult, ALU.add))
                v.reciprocal(tmp[:, 0:2, :], tmp[:, 0:2, :])
                lo(l, U_GR + 7)
                evac(v.reciprocal(tmp[:, 2:4, :], tmp[:, 2:4, :]), "var")
                lo(l, U_GL + 3)
                v.wait_ge(exp_ok, l * 3 + 3)
                for m in range(4):
                    ins = v.scalar_tensor_tensor(y[:, m, :], y[:, m, :], pr[:, C_GW + m:C_GW + m + 1], tmp[:, m, :], ALU.mult, ALU.mult)
                step(ins)
                lo(l, U_GL + 4)
                for m in range(4):
                    ins = v.scalar_tensor_tensor(y[:, m, :], y[:, m, :], pr[:, C_GB + m:C_GB + m + 1], bon[:, m, :], ALU.add, ALU.add)
                step(ins)
                v.tensor_tensor(ya, ya, gg, ALU.mult).then_inc(in_ok, 1)
                merge_gb(U_GL + 2)
                lo(l, U_GR + 10)
                lo(l, U_GR + 11)
                sub_split(l * (N_SPLIT + 1) + 6, sl[:, :, :], ya, sh[:, :, :])
                lo(l, U_GR + 12)
                v.wait_ge(a_free, a_at(l, U_BR - 1))
                for i in range(5):
                    if i < 4:
                        tiles = slice(2 * i, 2 * i + 2)
                        v.wait_ge(unit_done, done(l, U_BR + i))
                        v.tensor_tensor(gr[:, tiles, :], two((U_BR + i) % RING), gr[:, tiles, :], ALU.mult).then_inc(v_free, 1)
                        v.wait_ge(v_free, v_at(l, U_BR + i))
                        v.tensor_tensor(merged[:, tiles, :], merged[:, tiles, :], gr[:, tiles, :], ALU.add).then_inc(mg_ok, 1)
                    if i:
                        tiles = slice(2 * i - 2, 2 * i)
                        v.wait_ge(hh_ok, l * N_H + H_MG + i)
                        v.tensor_tensor(hl[:, tiles, :], merged[:, tiles, :], hh[:, tiles, :], ALU.subtract).then_inc(h_ok, 1)
                    if i < 4:
                        lo(l, U_BR + i + 2)
                for k in range(KT):
                    lo(l, U_WO + k + 2)
                    if k in (1, 6):
                        piece(l * 2 + 2, k // 6)
                    v.wait_ge(unit_done, done(l, U_WO + k))
                    v.scalar_tensor_tensor(x[:, k, :], ps[:, (U_WO + k) % RING, 0:SEQ], mod[:, 16 + k:17 + k], x[:, k, :],
                                           ALU.mult, ALU.add).then_inc(v_free, 1)
                v.wait_ge(v_free, v_at(l, U_WO + KT - 1))
                inv_square(l * N_NORM + 3, 3, 1, D_MODEL)
                norm(3, 24, H_N2)

                outer = base[0]

                def taps(j, r):
                    v.wait_ge(cv_ok, l * FT + j + 1)
                    for e in range(2):
                        src, dst = two(r)[:, e, :], cg[:, r, e, :]
                        step(v.scalar_tensor_tensor(dst[:, 1:], src[:, 0:SEQ - 1], pr[:, bass.ds(C_CW + (2 + e) * FT + j, 1)],
                                                    dst[:, 1:], ALU.mult, ALU.add))
                        v.scalar_tensor_tensor(dst[:, 2:], src[:, 0:SEQ - 2], pr[:, bass.ds(C_CW + e * FT + j, 1)],
                                               dst[:, 2:], ALU.mult, ALU.add).then_inc((cv2_ok, taps_ok)[e], 1)

                def multiply(j, r):
                    v.wait_ge(taps_ok, l * FT + j + 1 + 4)
                    v.wait_ge(si_ok, l * FT + j + 1)
                    v.tensor_tensor(sg[:, r, :], sg[:, r, :], cg[:, r, 1, :], ALU.mult).then_inc(mul_ok, 1)

                def act_lo(j, r):
                    v.wait_ge(ah_ok, l * FT + j + 1)
                    v.tensor_tensor(sl[:, r, :], sg[:, r, :], sh[:, r, :], ALU.subtract).then_inc(act_ok, 1)

                for j in range(2):
                    lo(l, U_FF + 2 * j + 2)
                    lo(l, U_FF + 2 * j + 3)
                    if j:
                        act_lo(0, 0)
                    taps(j, j)
                    multiply(j, j)
                per = 8
                with v.Fori(0, (FT - 2) // 4) as i:
                    base[0] = outer + i * per
                    start = count[0]
                    for o in range(4):
                        j, r = 2 + 4 * i + o, (2 + o) % 4

                        def lo_ff(e):
                            s = (U_FF + 3 * o + e) % RING
                            v.wait_ge(hi_ok, l * N_UNITS + i * 12 + U_FF + 6 + 3 * o + e + 1)
                            v.tensor_tensor(wl[:, s, :], raw[:, s, :], wh[:, s, :], ALU.subtract).then_inc(lo_ok, 1)

                        lo_ff(0)
                        lo_ff(1)
                        act_lo(j - 1, (r + 3) % 4)
                        taps(j, r)
                        lo_ff(2)
                        multiply(j, r)
                        if o == 2:
                            piece(l * 2 + 2, i + 2, first=False)
                    assert count[0] - start == per
                base[0] = outer
                count[0] += 4 * per
                piece(l * 2 + 2, 7)
                act_lo(FT - 1, (FT - 1) % 4)
                lo(l, N_UNITS)
                lo(l, N_UNITS + 1)
                mod_third(l * 3 + 3, 2, mod[:, 0:16], parall[:, 1, C_BADA:C_BADA + 16])
                gains(8, parall[:, 1, C_N1:C_N1 + KT])
                for k in range(KT):
                    if k == KT - 2:
                        v.wait_ge(unit_done, done(l, N_UNITS - 1))
                    elif k % 2 == 0:
                        v.wait_ge(dn_ps, l * 3 + k // 2 + 1)
                    v.scalar_tensor_tensor(x[:, k, :], two(4 + k // 2)[:, k % 2, :], mod[:, 40 + k:41 + k], x[:, k, :],
                                           ALU.mult, ALU.add).then_inc(x_ok, 1)
                inv_square(l * N_NORM + 4, 3, 1, D_MODEL)
            assert count[0] == N_DV, count[0]

            base[0], count[0] = DEPTH * N_DV + pre, 0
            v.wait_ge(rt_ok, DEPTH * N_NORM + 1)
            for k in range(KT):
                ins = v.scalar_tensor_tensor(sq[:, k, :], x[:, k, :], cn[:, K_FG + k:K_FG + k + 1], rs[:, 0, :], ALU.mult, ALU.mult)
            ins.then_inc(fin_ok, 1)

        @block.tensor
        def _(pe):
            def mm(o, lhsT, rhs_, start=True, stop=True):
                return pe.matmul(o, lhsT, rhs_, start=start, stop=stop)

            def mm3(o, lhs, rh, start, stop, skip=False):
                (lh, ll), (rh_, rl) = lhs, rh
                pe.matmul(o, lh, rh_, start=start, stop=False, skip_group_check=skip)
                pe.matmul(o, lh, rl, start=False, stop=False, skip_group_check=skip)
                return pe.matmul(o, ll, rh_, start=False, stop=stop, skip_group_check=skip)

            def weights(s, c, n=P, rows=slice(0, P)):
                return wh[rows, s, c:c + n], wl[rows, s, c:c + n]

            def wide(k, cols=slice(0, SEQ)):
                return hh[:, k, cols], hl[:, k, cols]

            def narrow(k, cols=slice(0, SEQ), rows=slice(0, P)):
                return sh[rows, k, cols], sl[rows, k, cols]

            def arrived(l, u):
                pe.wait_ge(lo_ok, l * N_UNITS + u + 1 + RING)

            def bank_free(l, u):
                if u in V_PLACE:
                    pe.wait_ge(v_free, v_at(l, u))
                else:
                    pe.wait_ge(a_free, a_at(l, u))

            def tile(s, half=None, ready=None):
                for k in range(KT) if half is None else range(half * 4, half * 4 + 4):
                    if ready:
                        ready(k)
                    last = mm3(ps[:, s, 0:SEQ], weights(s, k * P), wide(k), k == 0, k == KT - 1)
                return last

            def branch(s, j, ks=range(4)):
                for k in ks:
                    last = mm3(two(s)[:, j, :], weights(s, (j * 4 + k) * P), narrow(k), k == 0, k == 3)
                return last

            def mod_sum(bank, total):
                for m in range(16):
                    last = mm(ps[:, bank, m:m + 1], total[:, m * P:(m + 1) * P], ones[:, 0:1])
                last.then_inc(mod_ps, 1)

            def sumsq(nth):
                for k in range(KT):
                    pe.wait_ge(sqx_ok, nth * KT + k + 1)
                    last = mm(ps[:, 3, 0:SEQ], ones, sq[:, k, :], k == 0, k == KT - 1)
                last.then_inc(ss_ps, 1)

            sumsq(0)
            pe.wait_ge(ada_used, KT + 2)
            mod_sum(2, acc)
            with pe.Fori(0, DEPTH) as l:
                def rk(name):
                    return ev_at(l, name)

                with pe.Fori(0, 5) as i:
                    for s in range(RING):
                        pe.wait_ge(lo_ok, l * N_UNITS + i * RING + s + 1 + RING)
                        pe.wait_ge(a_free, l * N_A + i * RING + s + 1)
                        tile(s, ready=None if s else lambda k: pe.wait_ge(h_ok, l * N_H + k + 1)).then_inc(unit_done, 1)

                def full(u, ready=None):
                    arrived(l, u)
                    bank_free(l, u - RING)
                    tile(u % RING, ready=ready).then_inc(unit_done, 1)

                for u in range(15, 19):
                    full(u)
                arrived(l, U_LORA)
                bank_free(l, U_LORA - RING)
                pe.wait_ge(sl_ok, l * N_SPLIT + S_LORA)
                s = U_LORA % RING
                for m in range(4):
                    mm3(span(3)[:, m, :], weights(s, m * P, rows=slice(0, 64)), narrow(0, rows=slice(0, 64)), True, True)
                    mm3(span(5)[:, m, :], weights(s, m * P, rows=slice(64, 128)), narrow(0, rows=slice(64, 128)), True, True)
                for m in range(4):
                    last = mm3((two(7), two(s))[m // 2][:, m % 2, :], weights(s, 512 + m * P), narrow(1), True, True)
                last.then_inc(unit_done, 1)
                u = U_LORA + 1
                arrived(l, u)
                bank_free(l, u - RING)
                for m in range(4):
                    if m == 2:
                        pe.wait_ge(lora_ev, l * 10 + 2)
                    last = mm3((two(u % RING), two(3))[m // 2][:, m % 2, :], weights(u % RING, m * P, rows=slice(32, 64)),
                               narrow(2, rows=slice(32, 64)), True, True)
                last.then_inc(unit_done, 1)
                full(21)
                pe.wait_ge(kq_ok, l + 1)
                pe.wait_ge(lora_ev, l * 10 + 10)
                for e in range(2):
                    last = mm(ps[:, 5 + e, :], blk, sqk[:, 2 * e:2 * e + 2, :].rearrange("p a t -> p (a t)"))
                last.then_inc(rk_mm, 1)
                full(22)
                pe.wait_ge(sq_ok, l + 1)
                for k in range(4):
                    last = mm(two(7)[:, k // 2, :], ones, sq[:, k, :], k % 2 == 0, k % 2 == 1)
                last.then_inc(ss_ps, 1)
                full(23)
                full(24)
                pe.wait_ge(rk_ev, rk("ready"))
                for e in range(2):
                    last = mm(ps[:, 3 + e, :], blk, bon[:, 2 * e:2 * e + 2, :].rearrange("p a t -> p (a t)"))
                last.then_inc(rk_mm, 1)
                for u in range(25, U_FV):
                    if u == U_FV - 1:
                        pe.wait_ge(rec_ok, l * N_NORM + 2)
                        pe.wait_ge(ada_used, (l * 2 + 2) * KT + 2)
                        mod_sum(7, acc)
                    full(u)
                pe.wait_ge(rk_ev, rk("bon"))
                for e in range(2):
                    for i in range(2):
                        u = U_FV + 2 * e + i
                        arrived(l, u)
                        if i == 0:
                            bank_free(l, U_FV - 2 - e)
                        for b in range(TB):
                            for k in range(4):
                                last = mm3(ps[:, FV_BANKS[e][b], 0:256], wide(i * 4 + k, slice(b * P, (b + 1) * P)),
                                           weights(u % RING, k * 256, 256), i + k == 0, i * 4 + k == KT - 1, skip=True)
                        last.then_inc(unit_done, 1)
                pe.wait_ge(sl_ok, l * N_SPLIT + S_LAT)
                bank_free(l, U_FV + 3)
                for e in range(2):
                    u = U_QUP + e
                    arrived(l, u)
                    for hd in range(4):
                        for k in range(2):
                            last = mm3(span(5 - 2 * e)[:, hd, :], weights(u % RING, (k * 4 + hd) * P), narrow(k), k == 0, k == 1)
                    last.then_inc(unit_done, 1)
                arrived(l, U_KUP)
                bank_free(l, U_FV + 3)
                for m in range(4):
                    for k in range(2):
                        last = mm3(span(0)[:, m, :], weights(U_KUP % RING, k * 512 + m * P), narrow(2 + k), k == 0, k == 1)
                last.then_inc(unit_done, 1)
                arrived(l, U_VUP)
                pe.wait_ge(mod_ok, l * 3 + 2)
                for b in range(TB):
                    for k in range(2):
                        last = mm3(ps[:, (2, 7)[b], :], narrow(2 + k, slice(b * P, (b + 1) * P)), weights(U_VUP % RING, k * 512, 512), k == 0, k == 1)
                last.then_inc(unit_done, 1)
                pe.wait_ge(rope_ok, l * 2 + 2)
                pe.wait_ge(fl_dma, l * 32 + 32)
                pe.wait_ge(up_ok, l * 5 + 5)
                bank_free(l, U_FV + 3)
                alone(pe)

                def scores(n):
                    if n >= 3:
                        pe.wait_ge(s_ok, l * (2 * H) + n - 2)
                    for b in range(TB):
                        o = ps[:, n % 3, 128 * b:128 + 256 * b]
                        nk = P * (b + 1)
                        if n < H:
                            p0 = 64 * (n % 2)
                            mm(o, proj[p0:p0 + 64, T_FQ + n // 2, 1 + b * P:1 + (b + 1) * P],
                               proj[p0:p0 + 64, T_FK + n // 2, 1:1 + nk], True, False)
                            last = mm(o, fa[:, n, b * P:(b + 1) * P], fb[:, n, 0:nk], False, True)
                        else:
                            last = mm(o, qh[:, n - H, b * P:(b + 1) * P], kh[:, n - H, 0:nk])
                    last.then_inc(s_ps, 1)

                def transposed(n):
                    pe.wait_ge(pn_ok, l * (2 * H) + n + 1)
                    if n >= 2:
                        pe.wait_ge(pt_ok, l * (2 * H) + n - 1)
                    for j in range(3):
                        last = pe.transpose(ps[:, 3 + n % 2, j * P:(j + 1) * P], pp[:, n % 3, j * P:(j + 1) * P], ident)
                    last.then_inc(pt_ps, 1)

                def output(n):
                    pe.wait_ge(pt_ok, l * (2 * H) + n + 1)
                    if n >= 4:
                        pe.wait_ge(o_ok, l * H + n // 2 - 1)
                    vv = vf if n < H else vm
                    hd = n % H
                    o = ps[64 * (n % 2):64 * (n % 2) + 64, 5 + n // 2 % 2, 0:SEQ]
                    mm(o[:, 0:P], vv[:, 0, hd * 64:(hd + 1) * 64], pT[:, n % 2, 0:P])
                    mm(o[:, P:SEQ], vv[:, 0, hd * 64:(hd + 1) * 64], pT[:, n % 2, P:2 * P], True, False)
                    mm(o[:, P:SEQ], vv[:, 1, hd * 64:(hd + 1) * 64], pT[:, n % 2, 2 * P:3 * P], False, True).then_inc(o_ps, 1)

                scores(0)
                scores(1)
                for n in range(2 * H):
                    if n + 2 < 2 * H:
                        scores(n + 2)
                    transposed(n)
                    if n:
                        output(n - 1)
                pe.wait_ge(adb_used, l * (2 * H) + 2 * H + 2)
                mod_sum(7, acc2)
                output(2 * H - 1)
                pe.wait_ge(s_ok, l * (2 * H) + 2 * H)
                pe.wait_ge(o_ok, l * H + H)
                pe.wait_ge(rk_ev, rk("rho"))
                alone(pe)

                for g, (b, par_) in enumerate(GROUPS):
                    name = f"{b}{par_}"
                    rows = slice(64 * par_, 64 * par_ + 64)
                    t0 = b * P
                    u0 = U_GB + 6 * g

                    def half(n):
                        u, e = u0 + n // 2, n % 2
                        pair = (u - U_GB) % 3 == 2
                        if e == 0:
                            arrived(l, u)
                            if u >= U_GB + RING:
                                bank_free(l, u - RING)
                            if pair:
                                pe.wait_ge(sl_ok, l * N_SPLIT + (S_FOX if g < 2 else S_MLA))
                        last = branch(u % RING, e) if pair else tile(u % RING, e)
                        if e:
                            last.then_inc(unit_done, 1)

                    if par_ == 0:
                        if b:
                            pe.wait_ge(rk_ev, rk(f"tr{b}") - 1)
                            alone(pe)
                        for m in range(4):
                            for i, srcv in enumerate((ar[:, m, b, 0, :], bet[:, m, t0:t0 + P], kap[:, m, t0:t0 + P],
                                                      proj[:, T_V + m, 1 + t0:1 + t0 + P])):
                                last = pe.transpose(ps[:, 3 + i, m * P:(m + 1) * P], srcv, ident)
                        last.then_inc(rk_mm, 1)
                    if g:
                        pe.wait_ge(rk_ev, rk(f"WU{GROUPS[g - 1][0]}{GROUPS[g - 1][1]}"))
                    else:
                        pe.wait_ge(mod_ok, l * 3 + 3)
                    for m in range(4):
                        last = mm(four(7)[:, m, :], ar[rows, m, b, 0, :], bet[rows, m, t0:t0 + P])
                    last.then_inc(rk_mm, 1)
                    half(0)
                    if par_ == 0:
                        pe.wait_ge(tra_ok, l * TB + b + 1)
                    pe.wait_ge(rk_ev, rk(f"S{name}") - 1)
                    alone(pe)
                    for m in range(4):
                        arb = ar[rows, m, b, :, :].rearrange("p e t -> p (e t)")
                        mm(span(3)[:, m, :], kap[rows, m, t0:t0 + P], arb)
                        last = mm(span(5)[:, m, :], bet[rows, m, t0:t0 + P], arb)
                    last.then_inc(rk_mm, 1)
                    half(1)
                    for i in range(LV):
                        if i:
                            pe.wait_ge(t_ok, l * N_T + g * LV + i + (i > 1))
                        else:
                            pe.wait_ge(rk_ev, rk(f"S{name}"))
                        for m in range(4):
                            last = mm(four(7)[:, m, :], loT[:, m, :], tt[:, m, :])
                        last.then_inc(rk_mm, 1)
                        if g < 3 or i < 2:
                            half(2 + 2 * i)
                        if i == 0:
                            pe.wait_ge(m_ok, l * len(GROUPS) + g + 1)
                        pe.wait_ge(rk_ev, rk(f"X{name}{i}"))
                        if i < LV - 1:
                            for m in range(4):
                                last = mm(four(5)[:, m, :], ttT[:, m, :], xx[:, m, :])
                            last.then_inc(rk_mm, 1)
                        if i == 0:
                            for m in range(4):
                                hd = 2 * m + par_
                                mm(ps[:, 6, m * 64:(m + 1) * 64], lakT[:, m, :], toks[:, 3, hd * 64:(hd + 1) * 64])
                        for m in range(4):
                            last = mm(four(4)[:, m, :], xx[:, m, :], ttT[:, m, :])
                        last.then_inc(rk_mm, 1)
                        if i < LV - 1 and (g < 3 or i < 2):
                            half(3 + 2 * i)
                        elif g < 3:
                            branch((u0 + 5) % RING, 1, range(2))
                    pe.wait_ge(rk_ev, rk(f"TT{name}{LV - 1}"))
                    pe.wait_ge(t_ok, l * N_T + (g + 1) * LV)
                    for m in range(4):
                        last = mm(four(7)[:, m, :], ttT[:, m, :], rhs[:, m, :])
                    last.then_inc(rk_mm, 1)
                    if g < 3:
                        branch((u0 + 5) % RING, 1, range(2, 4)).then_inc(unit_done, 1)
                    pe.wait_ge(rk_ev, rk(f"WU{name}"))
                    alone(pe)
                    for m in range(4):
                        hd = 2 * m + par_
                        mm(four(3)[:, m, :], wu[:, m, :], mrbT[:, m, :], True, False)
                        last = mm(four(3)[:, m, :], v0n[:, hd, :], mrkT[:, m, :], False, True)
                        for c in range(2):
                            q = 2 * b + c
                            r = slice(64 * c, 64 * c + 64)
                            bt = toks[r, 1, hd * 64:(hd + 1) * 64]
                            kt = toks[r, 2, hd * 64:(hd + 1) * 64]
                            if q < NCH - 1:
                                o = ps[rows, 4 + c, m * 64:(m + 1) * 64]
                                mm(o, bt, wu[r, m, 64:128], True, False)
                                last = mm(o, kt, v0n[r, hd, 64:128], False, True)
                            if 0 < q < NCH - 1:
                                last = mm(ps[rows, 4 + c, 256 + m * 64:256 + (m + 1) * 64], wu[r, m, 0:64], bt)
                    last.then_inc(rk_mm, 1)
                filler = iter(range(U_GR, U_BR))
                full(next(filler))
                for q in range(1, NCH - 1):
                    pe.wait_ge(rk_ev, rk(f"st{q - 1}"))
                    alone(pe)
                    for m in range(4):
                        for p0 in (0, 64):
                            last = mm(ps[p0:p0 + 64, 3 + p0 // 64, m * 64:(m + 1) * 64], gT[p0:p0 + 64, q - 1, m, :], st[p0:p0 + 64, q - 1, m, :])
                    last.then_inc(rk_mm, 1)
                    full(next(filler))
                pe.wait_ge(rk_ev, rk("st2"))
                alone(pe)
                for m in range(4):
                    for q in range(1, NCH):
                        for p0 in (0, 64):
                            last = mm(span(3 + p0 // 32)[p0:p0 + 64, m, q * CHUNK:(q + 1) * CHUNK], st[p0:p0 + 64, q - 1, m, :],
                                      zT[p0:p0 + 64, m, (q - 1) * CHUNK:q * CHUNK])
                last.then_inc(rk_mm, 1)
                full(next(filler))
                pe.wait_ge(rk_ev, rk("y"))
                for e in range(2):
                    last = mm(ps[:, 3 + e, :], blk, y[:, 2 * e:2 * e + 2, :].rearrange("p a t -> p (a t)"))
                last.then_inc(rk_mm, 1)
                full(next(filler))
                pe.wait_ge(rk_ev, rk("mean"))
                for e in range(2):
                    last = mm(ps[:, 5 + e, :], blk, tmp[:, 2 * e:2 * e + 2, :].rearrange("p a t -> p (a t)"))
                last.then_inc(rk_mm, 1)
                for u in filler:
                    if u != U_GL + 2:
                        full(u)
                        continue
                    arrived(l, u)
                    bank_free(l, u - RING)
                    branch(u % RING, 0)
                    branch(u % RING, 1).then_inc(unit_done, 1)
                pe.wait_ge(sl_ok, l * N_SPLIT + S_RW)
                for i in range(4):
                    u = U_BR + i
                    arrived(l, u)
                    bank_free(l, u - RING)
                    for j in range(2):
                        last = branch(u % RING, j)
                    last.then_inc(unit_done, 1)
                full(U_WO, lambda k: pe.wait_ge(h_ok, l * N_H + H_MG + k // 2 + 1))
                for u in range(U_WO + 1, U_FF):
                    full(u)
                sumsq(l * 2 + 1)
                zero = cn[:, K_CAUS:K_CAUS + P]
                for b in range(4):
                    pe.matmul(ps[:, 4 + b, :], zero, cn[:, 0:512], start=True, stop=False, skip_group_check=True)

                def up(s, e, n, j, r, first=False):
                    pe.wait_ge(lo_ok, n + 1 + RING)
                    if e == 0:
                        pe.wait_ge(taps_ok, l * FT + j + 1)
                    for k in range(KT):
                        if first and e == 0:
                            pe.wait_ge(h_ok, l * N_H + H_N2 + k + 1)
                        last = mm3(two(r)[:, e, :], weights(s, k * P), wide(k), k == 0, k == KT - 1)
                    last.then_inc(unit_done, 1)

                def down(s, n, j, r, final=False):
                    pe.wait_ge(lo_ok, n + 1 + RING)
                    pe.wait_ge(act_ok, l * FT + j + 1)
                    for m in range(KT):
                        last = mm3(two(4 + m // 2)[:, m % 2, :], weights(s, m * P), narrow(r), False, final, skip=True)
                        if final and m in (1, 3, 5):
                            last.then_inc(dn_ps, 1)
                    last.then_inc(unit_done, 1)

                for j in range(2):
                    for e in range(2):
                        up((U_FF + 2 * j + e) % RING, e, l * N_UNITS + U_FF + 2 * j + e, j, j, j == 0)
                with pe.Fori(0, (FT - 2) // 4) as i:
                    for o in range(4):
                        j, r = 2 + 4 * i + o, (2 + o) % 4
                        n = l * N_UNITS + i * 12 + U_FF + 4 + 3 * o
                        for e in range(2):
                            up((U_FF + 4 + 3 * o + e) % RING, e, n + e, j, r)
                        down((U_FF + 6 + 3 * o) % RING, n + 2, j - 2, o)
                u = down_unit(FT - 2)
                down(u % RING, l * N_UNITS + u, FT - 2, (FT - 2) % 4)
                pe.wait_ge(ada_used, (l * 2 + 3) * KT + 2)
                mod_sum(2, acc)
                u += 1
                down(u % RING, l * N_UNITS + u, FT - 1, (FT - 1) % 4, final=True)
                sumsq(l * 2 + 2)


N_DV = 130


def _constants():
    c = np.zeros((P, N_CON), np.float32)
    i = np.arange(P)
    s, t = i[:, None], i[None, :]
    same = s // CHUNK == t // CHUNK
    c[:, K_ID:K_ID + P] = np.eye(P)
    c[:, K_ONES:K_ONES + SEQ] = 1
    c[:, K_BLK:K_BLK + P] = s // 64 == t // 64
    c[:, K_MS:K_MS + P] = same & (s < t)
    c[:, K_MI:K_MI + P] = same & (s <= t)
    c[:, K_N2T:K_N2T + P] = -1.0 * ((s // 2 == t // 2) & (s < t))
    c[:, K_N2:K_N2 + P] = -1.0 * ((s // 2 == t // 2) & (s > t))
    for n, w in enumerate(LEVELS):
        c[:, K_OFF + n * P:K_OFF + (n + 1) * P] = (s // (2 * w) == t // (2 * w)) & (s // w < t // w)
    c[:, K_CAUS + P:K_CAUS + 2 * P] = np.where(s >= t, 0, NEG)
    c[:, K_RST:K_RST + SEQ] = np.arange(SEQ)[None, :] % CHUNK != 0
    inv = np.power(np.float32(10000.0), -np.arange(16, dtype=np.float32) / np.float32(16))
    c[:, K_TRIG] = inv[i % 16]
    cos = i < 96
    c[:, K_TRIG + 1] = np.where(cos, 0.25, 0.0)
    c[:, K_TRIG + 2] = np.where(cos, np.pi / 2, 0.0)
    c[:, K_TRIG + 3] = np.where(cos | (i % 32 >= 16), 1.0, -1.0)
    return c


def _tiles(w):
    k, n = w.shape
    return w.reshape(k // P, P, n // P, P).transpose(1, 2, 0, 3)


def kernel(**inputs):
    import concourse.bacc as bacc
    from concourse.bass_utils import run_bass_kernel_spmd as run

    f = {k: np.asarray(v) for k, v in inputs.items()}
    cols = lambda v: v.reshape(-1, P).T
    units = np.zeros((DEPTH * N_UNITS + AHEAD, P, UNIT), np.float32)
    par = np.zeros((P, DEPTH, N_PAR), np.float32)
    for l in range(DEPTH):
        w = f["w_in"][l]
        put = lambda u, a: units[l * N_UNITS + u].__setitem__((slice(None), slice(0, a.reshape(P, -1).shape[1])), a.reshape(P, -1))
        r0, wl, k0, v0, al, gl = 0, 512, 576, 1088, 1600, 1664
        fq, fk, fv, ff, mq, mkv, mkr, gt = 1792, 2304, 2816, 3328, 3336, 3592, 3848, 3880
        mix = np.zeros((D_MODEL, P), np.float32)
        mix[:, 0:8] = w[:, ff:ff + 8]
        if l:
            mix[:, 32:64] = f["rw_vres_down"][l - 1]
        mix[:, 64:96] = w[:, mkr:mkr + 32]
        mix[:, 96:112], mix[:, 112:128] = w[:, mkr + 16:mkr + 32], w[:, mkr:mkr + 16]
        feat = np.concatenate([mix, w[:, wl:wl + 64], w[:, al:al + 64], w[:, gl:gl + 128], w[:, r0:r0 + 512],
                               w[:, k0:k0 + 512], w[:, v0:v0 + 512], w[:, mq:mq + 512], w[:, fq:fq + 1024]], 1)
        ft = _tiles(feat)
        for u in range(N_FEAT):
            put(u if u < U_LORA else u + 2, ft[:, u])
        for u in range(4):
            c, k = u // 2 * 256, u % 2 * 512
            put(U_FV + u, w[k:k + 512, fv + c:fv + c + 256].reshape(4, P, 256).transpose(1, 0, 2))
        lo = np.zeros((P, 2 * UNIT), np.float32)
        lo[0:64, 0:512], lo[64:128, 0:512] = f["rw_w_up"][l], f["rw_a_up"][l]
        lo[:, 512:1024] = f["rw_g_up"][l]
        if l:
            lo[32:64, 1024:1536] = f["rw_vres_up"][l - 1]
        put(U_LORA, lo[:, :UNIT])
        put(U_LORA + 1, lo[:, UNIT:])
        q = f["mla_w_q_up"][l].reshape(2, P, H, 96).transpose(1, 0, 2, 3)
        q = np.concatenate([q, q[..., 80:96], q[..., 64:80]], 3)
        put(U_QUP, q[:, :, 0:4])
        put(U_QUP + 1, q[:, :, 4:8])
        kv = f["mla_w_kv_up"][l].reshape(2, P, H, 2, 64).transpose(1, 0, 3, 2, 4)
        put(U_KUP, kv[:, :, 0])
        put(U_VUP, kv[:, :, 1])
        gw = _tiles(w[:, gt:gt + 3072])
        bt = [_tiles(f["w_branch"][l, g]) for g in range(3)]
        for g in (1, 2):
            for i in range(4):
                u = U_GB + ((g - 1) * 4 + i) * 3 if (g, i) < (2, 3) else U_GL
                put(u, gw[:, g * 8 + 2 * i])
                put(u + 1, gw[:, g * 8 + 2 * i + 1])
                put(u + 2, bt[g][:, 2 * i:2 * i + 2])
        for t in range(KT):
            put(U_GR + t if U_GR + t < U_GL else U_GR + t + 3, gw[:, t])
        for i in range(4):
            put(U_BR + i, bt[0][:, 2 * i:2 * i + 2])
        wo = _tiles(f["w_o"][l])
        for t in range(KT):
            put(U_WO + t, wo[:, t])
        up = _tiles(f["ffn_w_up"][l])
        dn = f["ffn_w_down"][l].reshape(FT, P, D_MODEL).transpose(1, 0, 2)
        for t in range(FT):
            put(up_unit(t), up[:, t])
            put(up_unit(t) + 1, up[:, FT + t])
            put(down_unit(t), dn[:, t])
        p = par[:, l]
        p[:, C_N1:C_N1 + 8], p[:, C_N2:C_N2 + 8] = cols(f["norm1_g"][l]), cols(f["norm2_g"][l])
        p[:, C_BADA:C_BADA + 48] = cols(f["b_ada"][l])
        mu = f["mu_shift"][l]
        p[:, C_MU + 1:C_MU + 15] = cols(np.concatenate([mu[wl:wl + 64], mu[al:al + 64], mu[gl:gl + 128], mu[r0:r0 + 512],
                                                        mu[k0:k0 + 512], mu[v0:v0 + 512]]))
        for c, name in ((C_W0, "rw_w0"), (C_A0, "rw_a0"), (C_KK, "rw_k_k"), (C_KA, "rw_k_a"), (C_RK, "rw_r_k"),
                        (C_GW, "rw_gn_w"), (C_GB, "rw_gn_b")):
            p[:, c:c + 4] = cols(f[name][l])
        p[0:8, C_MIX] = f["fox_b_f"][l]
        if l:
            p[:, C_V0:C_V0 + 4] = cols(f["rw_v0"][l - 1])
            p[32:64, C_MU] = f["rw_vres_mu"][l - 1]
        p[:, C_MQ:C_MQ + 2], p[:, C_MKV:C_MKV + 2] = cols(f["mla_q_norm_g"][l]), cols(f["mla_kv_norm_g"][l])
        p[:, C_FLAG], p[:, C_FLAG + 1] = float(l > 0), float(l == 0)
        p[:, C_CW:C_CW + 132] = f["ffn_conv_w"][l].reshape(3 * 2 * FT, P).T
        p[:, C_CB:C_CB + 44] = cols(f["ffn_conv_b"][l])
    con = _constants()
    con[:, K_FG:K_FG + 8] = cols(f["final_g"])
    wa = f["w_ada"].reshape(DEPTH, KT, P, 3, 2048).transpose(0, 3, 1, 2, 4).reshape(DEPTH * 3 * KT, P, 2048)
    wa = np.concatenate([wa, wa[:KT]], 0)
    arrays = {
        "xT": f["x"][0].T.reshape(KT, P, SEQ).transpose(1, 0, 2),
        "cT": cols(f["c"][0]),
        "pos": np.broadcast_to(f["positions"], (P, SEQ)),
        "par": par, "con": con, "wada": wa, "ws": units,
    }
    arrays = {k: np.ascontiguousarray(a) for k, a in arrays.items()}
    nc = bacc.Bacc("TRN2", target_bir_lowering=False, num_devices=1)
    args = [nc.dram_tensor(k, a.shape, mybir.dt.from_np(a.dtype), kind="ExternalInput").ap() for k, a in arrays.items()]
    args.append(nc.dram_tensor("out", (P, KT, SEQ), F32, kind="ExternalOutput").ap())
    bass_trunk(nc, *args)
    res = run(nc, [arrays], core_ids=[0]).results[0]["out"]
    return res.transpose(1, 0, 2).reshape(D_MODEL, SEQ).T.reshape(1, SEQ, D_MODEL)
```
